# Optimizing a Trainium2 kernel written in Bass

```python
import jax, jax.numpy as jnp
from jax import lax
import numpy as np

D_MODEL = 1024
BATCH = 1
SEQ = 512
DEPTH = 1

CTX_LEN = 256
GRID_W = 64

D_SSD = 1024
SSD_HEAD_DIM = 64
SSD_HEADS = D_SSD // SSD_HEAD_DIM
SSD_GROUPS = 4
SSD_HPG = SSD_HEADS // SSD_GROUPS
SSD_STATE = 128
SSD_CONV = 5
SSD_CHUNK = 128
D_CONV = 1024
SC_WIDTH = 3
D_MIX = D_SSD + D_CONV
XBC_DIM = D_SSD + 2 * SSD_GROUPS * SSD_STATE
IN_COLS = D_SSD + XBC_DIM + 2 * SSD_HEADS + 3 * D_CONV

PEER_HEADS = 8
PEER_N_KEYS = 128
PEER_N_EXPERTS = PEER_N_KEYS * PEER_N_KEYS
PEER_TOPK = 16
PEER_QUERY_DIM = 256
PEER_HALF = PEER_QUERY_DIM // 2
PEER_BLOCK = 128

N_MOD = 6
EPS = 1e-6

kernel_name = "hymba_ssd_shortconv_peer_prefix_block"

def rmsnorm(x, g):
    xf = x.astype(jnp.float32)
    y = xf * lax.rsqrt(jnp.mean(xf * xf, axis=-1, keepdims=True) + EPS)
    return y.astype(x.dtype) * g

def modulate(x, shift, scale):
    return x * (1 + scale) + shift

def dwconv_centred(u, w):
    K = w.shape[0]
    p = K // 2
    L = u.shape[-2]
    up = jnp.pad(u, [(0, 0)] * (u.ndim - 2) + [(p, p), (0, 0)])
    out = up[..., 0:L, :] * w[0]
    for k in range(1, K):
        out = out + up[..., k:k + L, :] * w[k]
    return out

def conv_rows(u, w):
    b, L, C = u.shape
    rows = L // GRID_W
    return dwconv_centred(u.reshape(b, rows, GRID_W, C), w).reshape(b, L, C)

def split_proj(proj):
    o = 0
    z = proj[..., o:o + D_SSD]; o += D_SSD
    xbc = proj[..., o:o + XBC_DIM]; o += XBC_DIM
    dt = proj[..., o:o + 2 * SSD_HEADS]; o += 2 * SSD_HEADS
    g_b = proj[..., o:o + D_CONV]; o += D_CONV
    g_c = proj[..., o:o + D_CONV]; o += D_CONV
    v = proj[..., o:o + D_CONV]
    return z, xbc, dt, g_b, g_c, v

def ssd_chunk_scan(xdt, a, bm, cm, h0):
    b, L, G, R, P = xdt.shape
    N = bm.shape[-1]
    Q = SSD_CHUNK
    nc = L // Q
    xdt = xdt.reshape(b, nc, Q, G, R, P)
    a = a.reshape(b, nc, Q, G, R)
    bm = bm.reshape(b, nc, Q, G, N)
    cm = cm.reshape(b, nc, Q, G, N)
    acs = jnp.cumsum(a, axis=2)
    lower = jnp.tril(jnp.ones((Q, Q), bool))[:, :, None, None]
    seg = acs[:, :, :, None] - acs[:, :, None, :]
    decay = jnp.exp(jnp.where(lower, seg, -jnp.inf))
    cb = jnp.einsum('bclgn,bcsgn->bclsg', cm, bm)
    y_diag = jnp.einsum('bclsg,bclsgr,bcsgrp->bclgrp', cb, decay, xdt)
    to_end = jnp.exp(acs[:, :, -1:] - acs)
    states = jnp.einsum('bclgn,bclgr,bclgrp->bcgrpn', bm, to_end, xdt)
    chunk_decay = jnp.exp(acs[:, :, -1])

    def step(h, inp):
        st, dec = inp
        return h * dec[..., None, None] + st, h

    h_final, h_enter = lax.scan(step, h0, (jnp.moveaxis(states, 1, 0), jnp.moveaxis(chunk_decay, 1, 0)))
    h_enter = jnp.moveaxis(h_enter, 0, 1)
    y_off = jnp.einsum('bclgn,bcgrpn,bclgr->bclgrp', cm, h_enter, jnp.exp(acs))
    return (y_diag + y_off).reshape(b, L, G, R, P), h_final

def ssd_prepare(xbc, dt_raw, conv_fn, conv_w, conv_b, dt_bias, a_log):
    xbc = jax.nn.silu(conv_fn(xbc, conv_w) + conv_b).astype(jnp.float32)
    b, L, _ = xbc.shape
    gn = SSD_GROUPS * SSD_STATE
    xs = xbc[..., :D_SSD].reshape(b, L, SSD_GROUPS, SSD_HPG, SSD_HEAD_DIM)
    bm = xbc[..., D_SSD:D_SSD + gn].reshape(b, L, SSD_GROUPS, SSD_STATE)
    cm = xbc[..., D_SSD + gn:].reshape(b, L, SSD_GROUPS, SSD_STATE)
    dt = jax.nn.softplus(dt_raw.astype(jnp.float32).reshape(b, L, 2, SSD_HEADS) + dt_bias.astype(jnp.float32))
    dt = dt.reshape(b, L, 2, SSD_GROUPS, SSD_HPG)
    a = dt * (-jnp.exp(a_log.astype(jnp.float32))).reshape(2, SSD_GROUPS, SSD_HPG)
    return xs, bm, cm, dt, a

def ssd_direction(xs, bm, cm, dt, a, h0, reverse):
    xdt = xs * dt[..., None]
    if reverse:
        xdt, a, bm, cm = jnp.flip(xdt, 1), jnp.flip(a, 1), jnp.flip(bm, 1), jnp.flip(cm, 1)
    y, h = ssd_chunk_scan(xdt, a, bm, cm, h0)
    if reverse:
        y = jnp.flip(y, 1)
    return y, h

def ssd_bidirectional(xs, bm, cm, dt, a, h0_fwd, h0_bwd):
    y_f, h_f = ssd_direction(xs, bm, cm, dt[:, :, 0], a[:, :, 0], h0_fwd, False)
    y_b, h_b = ssd_direction(xs, bm, cm, dt[:, :, 1], a[:, :, 1], h0_bwd, True)
    return y_f + y_b, h_f, h_b

def ssd_output(y, xs, z, d_skip, norm_g):
    b, L = y.shape[:2]
    y = y + d_skip.astype(jnp.float32).reshape(SSD_GROUPS, SSD_HPG)[..., None] * xs
    y = y.reshape(b, L, D_SSD) * jax.nn.silu(z.astype(jnp.float32))
    yg = y.reshape(b, L, SSD_GROUPS, D_SSD // SSD_GROUPS)
    yg = yg * lax.rsqrt(jnp.mean(yg * yg, axis=-1, keepdims=True) + EPS)
    return yg.reshape(b, L, D_SSD).astype(z.dtype) * norm_g

def shortconv_branch(g_b, g_c, v, conv_fn, w, norm_g):
    return rmsnorm(g_b * conv_fn(g_c * v, w), norm_g)

def token_mixer(h_lat, h_ctx, w_in, ssd_conv_w, ssd_conv_b, dt_bias, a_log, d_skip, ssd_norm_g,
                sc_conv_w, sc_norm_g, w_out, with_ctx_out):
    b = h_lat.shape[0]
    z_l, xbc_l, dt_l, gb_l, gc_l, v_l = split_proj(h_lat @ w_in)
    z_c, xbc_c, dt_c, gb_c, gc_c, v_c = split_proj(h_ctx @ w_in)
    xs_c, bm_c, cm_c, dtd_c, a_c = ssd_prepare(xbc_c, dt_c, dwconv_centred, ssd_conv_w, ssd_conv_b, dt_bias, a_log)
    h0 = jnp.zeros((b, SSD_GROUPS, SSD_HPG, SSD_HEAD_DIM, SSD_STATE), jnp.float32)
    y_c, hc_f, hc_b = ssd_bidirectional(xs_c, bm_c, cm_c, dtd_c, a_c, h0, h0)
    xs_l, bm_l, cm_l, dtd_l, a_l = ssd_prepare(xbc_l, dt_l, conv_rows, ssd_conv_w, ssd_conv_b, dt_bias, a_log)
    y_l, _, _ = ssd_bidirectional(xs_l, bm_l, cm_l, dtd_l, a_l, hc_f, hc_b)
    out_l = jnp.concatenate([ssd_output(y_l, xs_l, z_l, d_skip, ssd_norm_g),
                             shortconv_branch(gb_l, gc_l, v_l, conv_rows, sc_conv_w, sc_norm_g)], axis=-1) @ w_out
    out_c = None
    if with_ctx_out:
        out_c = jnp.concatenate([ssd_output(y_c, xs_c, z_c, d_skip, ssd_norm_g),
                                 shortconv_branch(gb_c, gc_c, v_c, dwconv_centred, sc_conv_w, sc_norm_g)], axis=-1) @ w_out
    return out_l, out_c

def peer(h, w_q, keys, u_tab, v_tab):
    b, L, D = h.shape
    tok = h.reshape(-1, PEER_BLOCK, D)

    def block(xb):
        T = xb.shape[0]
        q = (xb @ w_q).reshape(T, PEER_HEADS, 2, PEER_HALF)
        s = jnp.einsum('thpd,hpnd->thpn', q, keys).astype(jnp.float32)
        sv, si = lax.top_k(s, PEER_TOPK)
        cand = (sv[:, :, 0, :, None] + sv[:, :, 1, None, :]).reshape(T, PEER_HEADS, PEER_TOPK * PEER_TOPK)
        cv, ci = lax.top_k(cand, PEER_TOPK)
        i1 = jnp.take_along_axis(si[:, :, 0], ci // PEER_TOPK, axis=-1)
        i2 = jnp.take_along_axis(si[:, :, 1], ci % PEER_TOPK, axis=-1)
        eid = i1 * PEER_N_KEYS + i2
        g = jax.nn.softmax(cv, axis=-1).astype(xb.dtype)
        u = jnp.take(u_tab, eid, axis=0)
        act = jax.nn.gelu(jnp.einsum('thkd,td->thk', u, xb))
        return jnp.einsum('thk,thkd->td', g * act, jnp.take(v_tab, eid, axis=0))

    return lax.map(block, tok).reshape(b, L, D)

def setup_inputs(seed: int = 0) -> dict:
    key = jax.random.key(seed)
    ks = jax.random.split(key, 24)
    nrm = lambda k, shape, s: jax.random.normal(k, shape, jnp.float32) * s
    gain = lambda k, n: 1.0 + nrm(k, (DEPTH, n), 0.05)
    u = jax.random.uniform(ks[10], (DEPTH, 2, SSD_HEADS), jnp.float32)
    dt0 = jnp.exp(u * (np.log(0.1) - np.log(0.001)) + np.log(0.001)).astype(jnp.float32)
    dt_bias = dt0 + jnp.log(-jnp.expm1(-dt0))
    a_log = jnp.log(jax.random.uniform(ks[11], (DEPTH, 2, SSD_HEADS), jnp.float32, 1.0, 16.0))
    return {
        'x': nrm(ks[0], (BATCH, SEQ, D_MODEL), 1.0),
        'c': nrm(ks[1], (BATCH, D_MODEL), 1.0),
        'ctx': nrm(ks[2], (BATCH, CTX_LEN, D_MODEL), 1.0),
        'c_ctx': nrm(ks[3], (D_MODEL,), 1.0),
        'w_ada': nrm(ks[4], (DEPTH, D_MODEL, N_MOD * D_MODEL), 0.5 * D_MODEL ** -0.5),
        'b_ada': nrm(ks[5], (DEPTH, N_MOD * D_MODEL), 0.02),
        'g_pre_mix': gain(ks[6], D_MODEL),
        'g_post_mix': gain(ks[7], D_MODEL),
        'g_pre_ffn': gain(ks[8], D_MODEL),
        'g_post_ffn': gain(ks[9], D_MODEL),
        'w_in': nrm(ks[12], (DEPTH, D_MODEL, IN_COLS), D_MODEL ** -0.5),
        'ssd_conv_w': nrm(ks[13], (DEPTH, SSD_CONV, XBC_DIM), SSD_CONV ** -0.5),
        'ssd_conv_b': nrm(ks[14], (DEPTH, XBC_DIM), 0.02),
        'ssd_dt_bias': dt_bias,
        'ssd_a_log': a_log,
        'ssd_d': 1.0 + nrm(ks[15], (DEPTH, SSD_HEADS), 0.1),
        'ssd_norm_g': gain(ks[16], D_SSD),
        'sc_conv_w': nrm(ks[17], (DEPTH, SC_WIDTH, D_CONV), SC_WIDTH ** -0.5),
        'sc_norm_g': gain(ks[18], D_CONV),
        'w_out': nrm(ks[19], (DEPTH, D_MIX, D_MODEL), D_MIX ** -0.5),
        'peer_w_q': nrm(ks[20], (DEPTH, D_MODEL, PEER_HEADS * PEER_QUERY_DIM), D_MODEL ** -0.5),
        'peer_keys': nrm(ks[21], (DEPTH, PEER_HEADS, 2, PEER_N_KEYS, PEER_HALF), PEER_HALF ** -0.5),
        'peer_u': nrm(ks[22], (DEPTH, PEER_N_EXPERTS, D_MODEL), D_MODEL ** -0.5),
        'peer_v': nrm(ks[23], (DEPTH, PEER_N_EXPERTS, D_MODEL), D_MODEL ** -0.5),
    }

def reference(x, c, ctx, c_ctx, w_ada, b_ada, g_pre_mix, g_post_mix, g_pre_ffn, g_post_ffn,
              w_in, ssd_conv_w, ssd_conv_b, ssd_dt_bias, ssd_a_log, ssd_d, ssd_norm_g,
              sc_conv_w, sc_norm_g, w_out, peer_w_q, peer_keys, peer_u, peer_v):
    x_lat, x_ctx = x, ctx
    for layer in range(DEPTH):
        last = layer == DEPTH - 1
        mod_l = (jax.nn.silu(c) @ w_ada[layer] + b_ada[layer])[:, None, :]
        mod_c = jax.nn.silu(c_ctx) @ w_ada[layer] + b_ada[layer]
        sh1_l, sc1_l, gt1_l, sh2_l, sc2_l, gt2_l = jnp.split(mod_l, N_MOD, axis=-1)
        sh1_c, sc1_c, gt1_c, sh2_c, sc2_c, gt2_c = jnp.split(mod_c, N_MOD, axis=-1)
        h_l = modulate(rmsnorm(x_lat, g_pre_mix[layer]), sh1_l, sc1_l)
        h_c = modulate(rmsnorm(x_ctx, g_pre_mix[layer]), sh1_c, sc1_c)
        mix_l, mix_c = token_mixer(h_l, h_c, w_in[layer], ssd_conv_w[layer], ssd_conv_b[layer],
                                   ssd_dt_bias[layer], ssd_a_log[layer], ssd_d[layer], ssd_norm_g[layer],
                                   sc_conv_w[layer], sc_norm_g[layer], w_out[layer], not last)
        x_lat = x_lat + gt1_l * rmsnorm(mix_l, g_post_mix[layer])
        h2_l = modulate(rmsnorm(x_lat, g_pre_ffn[layer]), sh2_l, sc2_l)
        x_lat = x_lat + gt2_l * rmsnorm(peer(h2_l, peer_w_q[layer], peer_keys[layer], peer_u[layer], peer_v[layer]),
                                        g_post_ffn[layer])
        if not last:
            x_ctx = x_ctx + gt1_c * rmsnorm(mix_c, g_post_mix[layer])
            h2_c = modulate(rmsnorm(x_ctx, g_pre_ffn[layer]), sh2_c, sc2_c)
            x_ctx = x_ctx + gt2_c * rmsnorm(peer(h2_c, peer_w_q[layer], peer_keys[layer], peer_u[layer], peer_v[layer]),
                                            g_post_ffn[layer])
    return x_lat


_drawn_inputs = setup_inputs


def setup_inputs(seed=0):
    import zlib

    import numpy as np

    out = dict(_drawn_inputs(seed))
    spreads = {}
    factors = {'g_post_ffn': 3.797}
    for name, (base, spread) in spreads.items():
        noise = np.random.default_rng([zlib.crc32(name.encode()), seed]).standard_normal(out[name].shape)
        drawn = base * np.exp(spread * noise) if base else spread * noise
        out[name] = __import__('jax').numpy.asarray(drawn.astype(out[name].dtype))
    for name, factor in factors.items():
        out[name] = (out[name] * factor).astype(out[name].dtype)
    return out
```

```python
from contextlib import ExitStack

import concourse.bass as bass
from concourse import mybir

F32 = mybir.dt.float32
U32 = mybir.dt.uint32
ALU = mybir.AluOpType
ACT = mybir.ActivationFunctionType
AX = mybir.AxisListType.X

P = 128
EPS = 1e-6
KB = 256
CONV_K, SC_K = 5, 3
TOP = 16
NBANK = 8
GRID = 64
TINY = -3.0e38


def build(nc, x, c, ctx_in, c_ctx, w_ada, b_ada, g_pre_mix, g_post_mix, g_pre_ffn, g_post_ffn, w_in,
          conv_w, conv_b, dt_bias, a_log, d_skip, ssd_norm_g, sc_conv_w, sc_norm_g, w_out, w_q, keys,
          u_tab, v_tab, out):
    SEQ, D = x.shape[1], x.shape[2]
    CTX = ctx_in.shape[1]
    KD = D // P
    LT, CT = SEQ // P, CTX // P
    NT = LT + CT
    HEADS = dt_bias.shape[2]
    XBC = conv_w.shape[2]
    NXB = XBC // P
    NX = D // P
    NG = (NXB - NX) // 2
    HPG = HEADS // NG
    HD = D // HEADS
    GW = HPG * HD
    NCTX = NX + NG
    PH, NKEYS = keys.shape[1], keys.shape[3]
    NQ = 2 * PH
    NE = PH * TOP
    O_XBC, O_DT = D, D + XBC
    O_GB = O_DT + 2 * HEADS
    O_GC, O_V = O_GB + D, O_GB + 2 * D
    WCOL = 256
    WRING = 4

    plan = ["rowsA", "rowsB"] + [("ada1", g) for g in range(4)] + ["ada1T"]
    plan += [("hT", m, h) for m in range(NT) for h in range(2)]
    for ct in range(NXB):
        plan.append(("xl", ct))
        if ct < NCTX:
            plan.append(("xc", ct))
    plan.append("dt")
    plan += [("z", hq, m) for hq in range(4) for m in range(LT)]
    plan += [("xsT", m, h) for m in range(NT) for h in range(2)] + [("bT", m) for m in range(NT)]
    plan.append("acs")

    fwd = [("f", m) for m in range(LT, NT)] + [("f", m) for m in range(LT - 1)]
    bwd = [("b", m) for m in reversed(range(LT, NT))] + [("b", m) for m in reversed(range(1, LT))]
    steps = [s for pair in zip(fwd, bwd) for s in pair]
    projs = [(kind, ct) for ct in range(NX) for kind in ("gc", "v", "gb")]
    for g in range(8):
        projs.insert(8 * (g // 2) + 6 + g % 2, ("ada2", g))
    SCHED = [("x", 0), ("x", 1)]
    n_proj = 0

    def add_proj():
        nonlocal n_proj
        if n_proj < len(projs):
            SCHED.append(("proj", n_proj))
            if n_proj and projs[n_proj - 1][0] == "ada2":
                SCHED.append(("adaT", projs[n_proj - 1][1]))
            n_proj += 1

    for k in range(len(steps)):
        add_proj()
        SCHED.append(("step", k))
        if k + 2 < len(steps):
            SCHED.append(("x", k + 2))
    for m in range(LT):
        SCHED += [("cb", m), ("r", (m, 0))]
        for g in range(NG):
            SCHED.append(("m", (m, g)))
            add_proj()
            if g == 2:
                SCHED.append(("diag", (m, 0)))
            if g + 1 < NG:
                SCHED.append(("r", (m, g + 1)))
            SCHED.append(("y", (m, g)))
        SCHED += [("off", m), ("diag", (m, 1))]
        add_proj()
        SCHED.append(("out", m))
    while n_proj < len(projs):
        add_proj()
    SCHED.append(("adaT", 7))
    for kind, n in SCHED:
        if kind == "proj":
            plan.append(projs[n])
        elif kind == "adaT":
            plan.append(("ada2T", n))
        elif kind == "step":
            plan += [("st", n, 0), ("st", n, 1)]
        elif kind == "cb":
            plan.append(("cb", n))
        elif kind == "r":
            plan += [("rf", *n), ("rb", *n)]
        elif kind == "y" and n[1] % 2 == 0:
            plan.append(("y", n[0], n[1] // 2))
        elif kind == "off":
            plan += [(nm, n, h) for nm in ("of", "ob") for h in range(2)]
    plan.append("scsum")
    plan += [("row", r, h) for r in range(4) for h in range(2)]
    plan += [("yT", m, h) for m in range(LT) for h in range(2)]
    plan += [("wo", nq, part, tp) for tp in range(2) for nq in range(4) for part in range(2)]
    plan += [("kT", q4) for q4 in range(NQ // 4)]
    for m in range(LT):
        plan += [("h2T", m, h) for h in range(2)]
        for q4 in range(NQ // 4):
            plan.append(("q", m, q4))
        for q4 in range(NQ // 4):
            plan += [("qT", m, q4), ("s", m, q4)]
        if m:
            plan += [("vs", m - 1, h) for h in range(2)]
    plan += [("vs", LT - 1, h) for h in range(2)]
    unit = {name: n for n, name in enumerate(plan)}
    assert len(unit) == len(plan)

    with ExitStack() as stack:
        def sb(name, shape, dt=F32):
            return stack.enter_context(nc.sbuf_tensor(name, shape, dt))

        def sem(name):
            return stack.enter_context(nc.semaphore(name))

        arena = sb("arena", [P, 196 * KB])

        def at(kib, *dims):
            n = 1
            for d in dims:
                n *= d
            lo = int(kib * KB)
            v = arena[:, lo:lo + n]
            if len(dims) == 1:
                return v
            names = "abcd"[:len(dims)]
            return v.rearrange(f"p ({' '.join(names)}) -> p {' '.join(names)}", **dict(zip(names, dims)))

        wring = at(0, WRING, KD, WCOL)
        hTl, hTc = at(32, KD, SEQ), at(48, KD, CTX)
        xbl = at(56, NXB, SEQ)
        xbc_c = at(88, NCTX, CTX)
        zs = at(100, LT, D)
        scT = at(116, NX, SEQ)
        xin = at(164, NT, D)
        junk = at(100, NT, D)
        Bt = at(152, NT, NG * P)
        xs = at(164, NT, D)
        hf = at(56, LT, D)
        hb = at(132, LT, D)
        gcs, gcv, cv = at(88, 2, SEQ), at(92, 2, SEQ), at(96, 2, SEQ)
        sq, sqacc = at(148, SEQ), at(150, SEQ)
        atri = at(188, 4, HPG * P)
        mrow1 = at(140, 2 * D)
        xst = at(188, 2, D)
        xdt = at(180, 2, D)
        mdec = at(48, 4, HPG * P)
        yT = at(56, NX, SEQ)
        x1 = at(32, LT, D)
        mixes = at(132, LT, D)
        mix = [mixes[:, (m + 2) % LT] for m in range(LT)]
        sBt = at(152, 2, 512)
        ROW_GT1, ROW_GT2, ROW_SC2, ROW_SH2 = range(4)
        rows = [at(88, D), at(92, D), at(96, D), at(188, D)]
        h2 = at(164, LT, D)
        h2T = at(100, KD, SEQ)
        wqs = [wring[:, n] for n in range(WRING)] + [at(56 + 8 * n, KD, WCOL) for n in range(4)]
        h2Tt = at(142, KD, P)
        kraw = at(180, NQ, P)
        kTt = at(148, NQ, P)
        qt, qTt = at(124, 2, 512), at(128, 2, 4, P)
        scur = at(156, NQ, NKEYS)
        cand = at(132, PH, TOP * TOP)
        oh1, oh2 = at(140, TOP, TOP), at(141, TOP, TOP)
        vacc = at(188, 2, D)
        gslot = [at(100 + 4 * n, D) for n in range(6)] + [at(180 + 4 * n, D) for n in range(2)]
        NGS = len(gslot)
        NPE = NE // 2
        NDVE = NE + NE - NPE
        NDG = 4
        diag = at(146, NDG, P)

        ident, upper, lower, ones = (sb(n, [P, P]) for n in ("ident", "upper", "lower", "ones"))
        colA, colB = sb("colA", [P, P]), sb("colB", [P, P])
        rowA, rowB = at(132, P), at(133, P)
        A_CW, A_CB, A_NG, A_SG, A_C = 0, 80, 96, 104, 112
        B_SW, B_GPM, B_GQM, B_GPF, B_GQF, B_BA = 0, 24, 32, 40, 48, 56
        nB = 104
        cs = sb("cs", [P, 2, KD])
        mod1 = sb("mod1", [P, 2 * KD, 2])
        mod2 = sb("mod2", [P, 4 * KD])
        mrow2 = sb("mrow2", [2, 512])
        ssum, rstd = sb("ssum", [P, NT]), sb("rstd", [P, NT])
        wdt = sb("wdt", [P, KD, 2 * HEADS])
        dtb, alog, drow = sb("dtb", [P, 2 * HEADS]), sb("alog", [P, 2 * HEADS]), sb("drow", [P, HEADS])
        SM = [P, 2, NT, HEADS]
        adec, acs = sb("adec", SM), sb("acs", SM)
        dts, eacs, edec, wst = sb("dts", SM), sb("eacs", SM), sb("edec", SM), sb("wst", SM)
        dtx, dta, dte, dtu, dtl, tot = (at(132 + n, 2, NT, HEADS) for n in range(6))
        gss, grs = sb("gss", [P, LT * NG]), sb("grs", [P, LT * NG])
        scss, mss, mrs = sb("scss", [P, LT]), sb("mss", [P, LT]), sb("mrs", [P, LT])
        xss, xrs = sb("xss", [P, LT]), sb("xrs", [P, LT])
        epsc, modr = sb("epsc", [P, 1]), sb("modr", [P, 4 * KD])
        yacc, yoff = at(152, D), at(156, D)
        cbm = at(160, 2, NG, P)
        h2c = at(48, D)
        iota_j, iota_i = sb("iota_j", [P, TOP]), sb("iota_i", [P, TOP], mybir.dt.int32)

        def small(half_kib, *dims, dt=F32):
            v = at(half_kib / 2, *dims)
            return v if dt == F32 else v.bitcast(dt)

        sv, si = small(176, NQ, TOP), small(178, NQ, TOP, dt=U32)
        cva, cia = small(182, PH, TOP), small(183, PH, TOP, dt=U32)
        ka, kb = small(192, PH, TOP, dt=U32), small(193, PH, TOP, dt=U32)
        e1, e2 = small(196, PH, TOP), small(197, PH, TOP)
        eidn, gaten = small(198, PH * TOP, dt=U32), small(199, PH, TOP)
        eid, gate = small(104, PH * TOP, dt=U32), small(105, PH * TOP)
        dots, wexp = small(106, PH * TOP), small(107, PH * TOP)
        gsum, ginv = small(194, PH), small(195, PH)
        fss, frs = sb("fss", [P, 1]), sb("frs", [P, 1])

        bank = [stack.enter_context(nc.psum_tensor(f"bank{i}", [P, 512], F32)) for i in range(NBANK)]
        full = [sem(f"bank{i}_full") for i in range(NBANK)]
        free = [sem(f"bank{i}_free") for i in range(NBANK)]

        s_rows, s_vec, s_x = sem("vector_rows_loaded"), sem("row_vectors_loaded"), sem("tokens_loaded")
        s_w = [sem(f"weights{i}_loaded") for i in range(WRING)]
        s_wused = sem("ada_weights_used")
        s_wq = [sem(f"query_weights{i}_loaded") for i in range(4)]
        s_atri = sem("log_decays_masked")
        s_wdt, s_x1, s_keys = sem("dt_weights_loaded"), sem("tokens_reloaded"), sem("keys_loaded")
        s_cst2, s_const, s_dti = sem("constants_filled"), sem("constants_built"), sem("eps_set")
        s_cs, s_mod1 = sem("silu_c_ready"), sem("mod1_ready")
        s_ss, s_sqrt, s_xn = sem("squares_summed"), sem("x_root_ready"), sem("x_normed")
        s_xb = sem("xbc_ready")
        s_dtx, s_dte, s_dtl = sem("dt_biased"), sem("dt_exp"), sem("dt_log")
        s_a, s_acs, s_edec = sem("decay_ready"), sem("acs_ready"), sem("decays_exp")
        s_xst, s_xdt = sem("xst_ready"), sem("xdt_ready")
        s_sq, s_sqa = sem("sc_squared"), sem("sc_squares_added")
        s_dec, s_m, s_mu, s_y = sem("decay_exp"), sem("mdec_ready"), sem("mdec_used"), sem("y_ready")
        s_gss, s_groot, s_yn = sem("group_squares"), sem("group_root"), sem("y_normed")
        s_scr, s_scn, s_mod2 = sem("sc_root"), sem("sc_normed"), sem("mod2_ready")
        s_mss, s_mr, s_x1n = sem("mix_squares"), sem("mix_root"), sem("x1_ready")
        s_xss, s_xr, s_h2 = sem("x1_squares"), sem("x1_root"), sem("h2_ready")
        s_scur, s_cv, s_ge = sem("scores_staged"), sem("candidates_ranked"), sem("gate_exp")
        s_pick, s_eid = sem("experts_picked"), sem("expert_ids_ready")
        s_gsl = [sem(f"row{i}_landed") for i in range(NGS)]
        s_used, s_gelu = sem("row_used"), sem("gelu_ready")
        s_wexp, s_diag, s_peused = sem("weights_ready"), sem("diagonal_ready"), sem("row_multiplied")
        s_fss, s_froot, s_fin, s_out = sem("out_squares"), sem("out_root"), sem("out_ready"), sem("out_stored")
        s_dve, s_gate, s_pgate = sem("dve_step"), sem("dve_wait_passed"), sem("pool_wait_passed")

        def hT_tile(m, k):
            a, i = (hTl, m) if m < LT else (hTc, m - LT)
            return a[:, k, i * P:(i + 1) * P]

        def bank_of(name):
            return bank[unit[name] % NBANK]

        def claim(name):
            u = unit[name]
            if u >= NBANK:
                nc.tensor.wait_ge(free[u % NBANK], u // NBANK)
            return bank[u % NBANK]

        def filled(ins, name):
            ins.then_inc(full[unit[name] % NBANK], 1)

        def release(ins, name):
            ins.then_inc(free[unit[name] % NBANK], 1)

        def await_read(eng, name):
            u = unit[name]
            eng.wait_ge(free[u % NBANK], u // NBANK + 1)

        def await_filled(eng, name):
            u = unit[name]
            eng.wait_ge(full[u % NBANK], u // NBANK + 1)

        def await_bank(eng, name):
            await_filled(eng, name)
            return bank_of(name)

        loads, users = [], []

        def add_load(w, off, j, user):
            loads.append((w, off, j))
            users.append(user)

        N_ADA1, N_ADA2 = 2 * D // WCOL, 4 * D // WCOL
        for n in range(N_ADA1):
            add_load(w_ada[0], 0, n, ("ada1", n // 2) if n % 2 else n // 2 + 1)
        xbc_0 = len(loads)
        for n in range(XBC // WCOL):
            ct = 2 * n + 1
            add_load(w_in[0], O_XBC, n, ("xc" if ct < NCTX else "xl", ct))
        z_0 = len(loads)
        for n in range(D // WCOL):
            add_load(w_in[0], 0, n, ("z", n, LT - 1))
        proj_load = {}
        for kind, n in projs:
            if kind == "ada2":
                proj_load[kind, n] = len(loads)
                add_load(w_ada[0], 2 * D, 2 * n, N_ADA1 // 2 + n + 1)
                add_load(w_ada[0], 2 * D, 2 * n + 1, (kind, n))
            elif n % 2 == 0:
                proj_load[kind, n] = proj_load[kind, n + 1] = len(loads)
                add_load(w_in[0], {"gc": O_GC, "v": O_V, "gb": O_GB}[kind], n // 2, (kind, n + 1))
        wo_0 = len(loads)
        for tp in range(2):
            for n in range(D // WCOL):
                for part in range(2):
                    add_load(w_out[0][part * D:(part + 1) * D], 0, n, ("wo", n, part, tp))
        wq_0 = len(loads)
        for n in range(WRING):
            add_load(w_q[0], 0, n, None)

        block = stack.enter_context(nc.Block())

        @block.sync
        def _(sp):
            rA = [(A_CW, conv_w[0].rearrange("k (c p) -> (k c) p", p=P)),
                  (A_CB, conv_b.rearrange("a (c p) -> (a c) p", p=P)),
                  (A_NG, ssd_norm_g.rearrange("a (c p) -> (a c) p", p=P)),
                  (A_SG, sc_norm_g.rearrange("a (c p) -> (a c) p", p=P)),
                  (A_C, c.rearrange("a (c p) -> (a c) p", p=P)),
                  (A_C + KD, c_ctx.rearrange("(c p) -> c p", p=P))]
            rB = [(B_SW, sc_conv_w[0].rearrange("k (c p) -> (k c) p", p=P)),
                  (B_GPM, g_pre_mix.rearrange("a (c p) -> (a c) p", p=P)),
                  (B_GQM, g_post_mix.rearrange("a (c p) -> (a c) p", p=P)),
                  (B_GPF, g_pre_ffn.rearrange("a (c p) -> (a c) p", p=P)),
                  (B_GQF, g_post_ffn.rearrange("a (c p) -> (a c) p", p=P)),
                  (B_BA, b_ada.rearrange("a (c p) -> (a c) p", p=P))]
            for dst, srcs in ((rowA, rA), (rowB, rB)):
                for r, src in srcs:
                    sp.dma_start(dst[r:r + src.shape[0], :], src).then_inc(s_rows, 16)
            for n, (w, off, j) in enumerate(loads):
                if n >= WRING:
                    user = users[n - WRING]
                    if isinstance(user, int):
                        sp.wait_ge(s_wused, user)
                    else:
                        await_filled(sp, user)
                src = w[:, off + j * WCOL:off + (j + 1) * WCOL].rearrange("(k p) n -> p k n", p=P)
                sp.dma_start(wring[:, n % WRING], src).then_inc(s_w[n % WRING], 16)
            await_filled(sp, ("wo", 3, 1, 1))
            for n in range(WRING, 2 * WRING):
                src = w_q[0][:, n * WCOL:(n + 1) * WCOL].rearrange("(k p) n -> p k n", p=P)
                sp.dma_start(wqs[n], src).then_inc(s_wq[n - WRING], 16)

        @block.gpsimd
        def _(pool):
            nc.gpsimd.memset(ident[:], 0.0).then_inc(s_cst2, 1)
            nc.gpsimd.memset(upper[:], 1.0).then_inc(s_cst2, 1)
            nc.gpsimd.memset(lower[:], 1.0).then_inc(s_cst2, 1)
            nc.gpsimd.memset(ones[:], 1.0).then_inc(s_cst2, 1)
            nc.gpsimd.iota(iota_i[:], pattern=[[1, TOP]], base=0, channel_multiplier=0).then_inc(s_cst2, 1)
            pool.wait_ge(s_cst2, 5)
            nc.gpsimd.affine_select(out=ident[:], in_=ident[:], compare_op=ALU.not_equal, fill=1.0, base=0,
                                    pattern=[[-1, P]], channel_multiplier=1).then_inc(s_const, 1)
            nc.gpsimd.affine_select(out=upper[:], in_=upper[:], compare_op=ALU.is_ge, fill=0.0, base=0,
                                    pattern=[[1, P]], channel_multiplier=-1).then_inc(s_const, 1)
            nc.gpsimd.affine_select(out=lower[:], in_=lower[:], compare_op=ALU.is_ge, fill=0.0, base=0,
                                    pattern=[[-1, P]], channel_multiplier=1).then_inc(s_const, 1)
            nc.gpsimd.tensor_copy(iota_j[:], iota_i[:]).then_inc(s_const, 1)
            for kind, n in SCHED:
                if kind == "r":
                    m, g = n
                    b = m * NG + g
                    if b == 0:
                        await_filled(pool, ("st", len(steps) - 1, 1))
                    for d, tri in enumerate((upper, lower)):
                        if b >= 2:
                            await_filled(pool, (("rf", "rb")[d], (b - 2) // NG, (b - 2) % NG))
                        nc.gpsimd.tensor_tensor(
                            atri[:, (2 * b + d) % 4].rearrange("p (r l) -> p r l", l=P),
                            tri[:].unsqueeze(1).to_broadcast([P, HPG, P]),
                            adec[:, d, m, g * HPG:(g + 1) * HPG].unsqueeze(2).to_broadcast([P, HPG, P]),
                            ALU.mult).then_inc(s_atri, 1)
                elif kind == "proj" and projs[n][0] == "gb":
                    ct = projs[n][1]
                    await_read(pool, ("gb", ct))
                    if ct == 0:
                        nc.gpsimd.tensor_tensor(sqacc, scT[:, 0], scT[:, 0], ALU.mult).then_inc(s_sqa, 1)
                    else:
                        if ct >= 2:
                            pool.wait_ge(s_sqa, ct)
                        nc.gpsimd.tensor_tensor(sq, scT[:, ct], scT[:, ct], ALU.mult).then_inc(s_sq, 1)
                        pool.wait_ge(s_sq, ct)
                        pool.wait_ge(s_sqa, ct)
                        nc.gpsimd.tensor_tensor(sqacc, sqacc, sq, ALU.add).then_inc(s_sqa, 1)

            await_filled(pool, ("gb", NX - 1))
            pool.dma_start(x1, x[0].rearrange("(m p) d -> p m d", p=P)).then_inc(s_x1, 16)
            pool.wait_ge(s_gss, LT * NG)
            pool.dma_start(kraw, keys[0].rearrange("h q n d -> n (h q) d")).then_inc(s_keys, 16)


            await_filled(pool, ("wo", 3, 1, 1))
            await_filled(pool, ("kT", NQ // 4 - 1))

            def tile(t, first):
                if not first:
                    pool.wait_ge(s_eid, t + PH)
                    nc.gpsimd.sem_inc(s_pgate, 1)
                for half, tab in enumerate((u_tab[0], v_tab[0])):
                    for k in range(NE):
                        n = half * NE + k
                        if first and n < NE and n % TOP == 0:
                            pool.wait_ge(s_eid, n // TOP + 1)
                            nc.gpsimd.sem_inc(s_pgate, 1)
                        if not (first and n < NGS):
                            o = n - NGS
                            if o < 0 and n % 2:
                                pool.wait_ge(s_peused, t * NPE + (o + 1) // 2)
                            elif o < 0:
                                pool.wait_ge(s_used, t * NDVE + (o + 2) // 2)
                            elif o < NE:
                                pool.wait_ge(s_used, t * NDVE + o + 1)
                            elif o % 2:
                                pool.wait_ge(s_peused, t * NPE + (o - NE) // 2 + 1)
                            else:
                                pool.wait_ge(s_used, t * NDVE + NE + (o - NE) // 2 + 1)
                            nc.gpsimd.sem_inc(s_pgate, 1)
                        nc.gpsimd.indirect_dma_start(
                            gslot[n % NGS], None, tab, bass.IndirectOffsetOnAxis(eid[:, k:k + 1], 0)
                        ).then_inc(s_gsl[n % NGS], 16)

            tile(0, True)
            with pool.Fori(1, LT) as t:
                tile(t, False)

        @block.tensor
        def _(pe):
            mm, tr = nc.tensor.matmul, nc.tensor.transpose

            def weights(n):
                pe.wait_ge(s_w[n % WRING], 16 * (n // WRING + 1))
                return wring[:, n % WRING]

            pe.wait_ge(s_const, 1)
            pe.wait_ge(s_rows, 12 * 16)
            filled(tr(claim("rowsA")[:, 0:P], rowA, ident[:]), "rowsA")
            filled(tr(claim("rowsB")[:, 0:nB], rowB[0:nB, :], ident[0:nB, 0:nB]), "rowsB")

            def ada(name, first, lhs, rows_):
                ps = claim(name)
                for i in range(2):
                    w = weights(first + i)
                    for k in range(KD):
                        last = mm(ps[0:rows_, i * WCOL:(i + 1) * WCOL], lhs(k), w[:, k, :],
                                  start=(k == 0), stop=(k == KD - 1))
                    if i == 0:
                        last.then_inc(s_wused, 1)
                filled(last, name)

            pe.wait_ge(s_cs, 1)
            for g in range(4):
                ada(("ada1", g), 2 * g, lambda k: cs[:, :, k], 2)
            ps = claim("ada1T")
            await_read(pe, ("ada1", 3))
            for j in range(2 * KD):
                last = tr(ps[:, 2 * j:2 * j + 2], mrow1[0:2, j * P:(j + 1) * P], ident[0:2, 0:2])
            filled(last, "ada1T")

            for m in range(NT):
                pe.wait_ge(s_xn, m + 1)
                for h in range(2):
                    ps = claim(("hT", m, h))
                    for k in range(4):
                        last = tr(ps[:, k * P:(k + 1) * P], xin[:, m, (4 * h + k) * P:(4 * h + k + 1) * P], ident[:])
                    filled(last, ("hT", m, h))
            await_read(pe, ("hT", NT - 1, 0))
            await_read(pe, ("hT", NT - 1, 1))

            def project_T(name, w, j, hT, n):
                ps = claim(name)
                for k in range(KD):
                    last = mm(ps[:, 0:n], w[:, k, j * P:(j + 1) * P], hT[:, k, :],
                              start=(k == 0), stop=(k == KD - 1))
                filled(last, name)
                return last

            for n in range(XBC // WCOL):
                w = weights(xbc_0 + n)
                for j in range(2):
                    ct = 2 * n + j
                    project_T(("xl", ct), w, j, hTl, SEQ)
                    if ct < NCTX:
                        project_T(("xc", ct), w, j, hTc, CTX)

            ps = claim("dt")
            pe.wait_ge(s_wdt, 16)
            for m in range(NT):
                for k in range(KD):
                    last = mm(ps[:, m * 2 * HEADS:(m + 1) * 2 * HEADS], hT_tile(m, k), wdt[:, k, :],
                              start=(k == 0), stop=(k == KD - 1))
            filled(last, "dt")

            for hq in range(4):
                w = weights(z_0 + hq)
                for m in range(LT):
                    ps = claim(("z", hq, m))
                    for k in range(KD):
                        last = mm(ps[:, 0:WCOL], hT_tile(m, k), w[:, k, :],
                                  start=(k == 0), stop=(k == KD - 1))
                    filled(last, ("z", hq, m))

            pe.wait_ge(s_xb, NXB + NCTX)
            for m in range(NT):
                src, lo = (xbl, m * P) if m < LT else (xbc_c, (m - LT) * P)
                for h in range(2):
                    ps = claim(("xsT", m, h))
                    for k in range(4):
                        last = tr(ps[:, k * P:(k + 1) * P], src[:, 4 * h + k, lo:lo + P], ident[:])
                    filled(last, ("xsT", m, h))
            for m in range(NT):
                src, lo = (xbl, m * P) if m < LT else (xbc_c, (m - LT) * P)
                ps = claim(("bT", m))
                for g in range(NG):
                    last = tr(ps[:, g * P:(g + 1) * P], src[:, NX + g, lo:lo + P], ident[:])
                filled(last, ("bT", m))

            pe.wait_ge(s_a, 1)
            pe.wait_ge(s_const, 4)
            ps = claim("acs")
            NA = NT * HEADS
            ad = adec[:].rearrange("p d m h -> p (d m h)")
            mm(ps[:, 0:NA], upper[:], ad[:, 0:NA], start=True, stop=True)
            mm(ps[:, NA:2 * NA], lower[:], ad[:, NA:2 * NA], start=True, stop=True)
            filled(mm(ps[:, 2 * NA:4 * NA], ones[:], ad, start=True, stop=True), "acs")
            await_read(pe, ("bT", NT - 1))

            def proj(n):
                kind, ct = projs[n]
                if kind == "ada2":
                    ada((kind, ct), proj_load[kind, ct], lambda k: cs[:, :, k], 2)
                else:
                    project_T((kind, ct), weights(proj_load[kind, ct]), ct % 2, hTl, SEQ)

            def step(k):
                d, m = steps[k]
                pe.wait_ge(s_xst, k + 1)
                for h in range(2):
                    ps = claim(("st", k, h))
                    for g in range(2):
                        gg = 2 * h + g
                        last = mm(ps[:, g * GW:(g + 1) * GW], Bt[:, m, gg * P:(gg + 1) * P],
                                  xst[:, k % 2, gg * GW:(gg + 1) * GW], start=True, stop=True)
                    filled(last, ("st", k, h))

            def c_times_b(m):
                ps = claim(("cb", m))
                for g in range(NG):
                    last = mm(ps[:, g * P:(g + 1) * P], xbl[:, NX + g, m * P:(m + 1) * P],
                              xbl[:, NX + NG + g, m * P:(m + 1) * P], start=True, stop=True)
                filled(last, ("cb", m))

            def decay_sums(mg):
                m, g = mg
                for d, nm in enumerate(("rf", "rb")):
                    ps = claim((nm, m, g))
                    b = m * NG + g
                    pe.wait_ge(s_atri, 2 * b + d + 1)
                    filled(mm(ps[:, :], ones[:], atri[:, (2 * b + d) % 4], start=True, stop=True), (nm, m, g))

            def diagonal(mg):
                m, g = mg
                b = m * NG + g
                name = ("y", m, g // 2)
                yps = claim(name) if g % 2 == 0 else bank_of(name)
                pe.wait_ge(s_m, 2 * (b + 1))
                pe.wait_ge(s_xdt, 2 * (m + 1))
                for r in range(HPG):
                    h = g * HPG + r
                    col = (h % 8) * HD
                    for d in range(2):
                        last = mm(yps[:, col:col + HD], mdec[:, (2 * b + d) % 4, r * P:(r + 1) * P],
                                  xdt[:, d, h * HD:(h + 1) * HD], start=(d == 0), stop=(d == 1))
                if g % 2:
                    filled(last, name)
                else:
                    last.then_inc(s_mu, 1)

            def entering(m):
                await_read(pe, ("st", len(steps) - 1, 1))
                for nm, hs in (("of", hf), ("ob", hb)):
                    for h in range(2):
                        ps = claim((nm, m, h))
                        for g in range(2):
                            gg = 2 * h + g
                            last = mm(ps[:, g * GW:(g + 1) * GW], xbl[:, NX + NG + gg, m * P:(m + 1) * P],
                                      hs[:, m, gg * GW:(gg + 1) * GW], start=True, stop=True)
                        filled(last, (nm, m, h))

            def ada_T(g):
                ps = claim(("ada2T", g))
                await_read(pe, ("ada2", g))
                for j in range(4):
                    last = tr(ps[:, 2 * j:2 * j + 2], mrow2[0:2, j * P:(j + 1) * P], ident[0:2, 0:2])
                filled(last, ("ada2T", g))

            parts = {"proj": proj, "adaT": ada_T, "step": step, "cb": c_times_b, "r": decay_sums, "y": diagonal, "off": entering}
            for kind, n in SCHED:
                if kind in parts:
                    parts[kind](n)

            ps = claim("scsum")
            pe.wait_ge(s_sqa, NX)
            for m in range(LT):
                last = mm(ps[:, m:m + 1], sqacc[:, m * P:(m + 1) * P], ones[:, 0:1], start=True, stop=True)
            filled(last, "scsum")

            pe.wait_ge(s_mod2, 1)
            for r in range(4):
                for h in range(2):
                    ps = claim(("row", r, h))
                    for k in range(4):
                        j = r * KD + 4 * h + k
                        last = mm(ps[:, k * P:(k + 1) * P], mod2[:, j:j + 1].to_broadcast([P, P]), ident[:],
                                  start=True, stop=True)
                    filled(last, ("row", r, h))

            for m in range(LT):
                pe.wait_ge(s_yn, m + 1)
                for h in range(2):
                    ps = claim(("yT", m, h))
                    for k in range(4):
                        last = tr(ps[:, k * P:(k + 1) * P], zs[:, m, (4 * h + k) * P:(4 * h + k + 1) * P], ident[:])
                    filled(last, ("yT", m, h))
            await_read(pe, ("yT", LT - 1, 1))
            pe.wait_ge(s_scn, 1)

            for tp in range(2):
                for nq in range(4):
                    for part, src in enumerate((yT, scT)):
                        w = weights(wo_0 + 8 * tp + 2 * nq + part)
                        ps = claim(("wo", nq, part, tp))
                        for i in range(2):
                            m = 2 * tp + i
                            for k in range(KD):
                                last = mm(ps[:, i * WCOL:(i + 1) * WCOL], src[:, k, m * P:(m + 1) * P], w[:, k, :],
                                          start=(k == 0), stop=(k == KD - 1))
                        filled(last, ("wo", nq, part, tp))

            pe.wait_ge(s_keys, 16)
            for q4 in range(NQ // 4):
                ps = claim(("kT", q4))
                for k in range(4):
                    last = tr(ps[:, k * P:(k + 1) * P], kraw[:, 4 * q4 + k, :], ident[:])
                filled(last, ("kT", q4))

            def add_rows(m):
                acc = [claim(("vs", m, h)) for h in range(2)]
                for i in range(NPE):
                    n = NE + 2 * i + 1
                    s = n % NGS
                    pe.wait_ge(s_diag, m * NPE + i + 1)
                    pe.wait_ge(s_gsl[s], 16 * (m * (2 * NE // NGS) + n // NGS + 1))
                    for h in range(2):
                        last = mm(acc[h][:, :], diag[:, i % NDG], gslot[s][:, h * 512:(h + 1) * 512],
                                  start=(i == 0), stop=(i == NPE - 1))
                        if i == NPE - 1 and h == 0:
                            filled(last, ("vs", m, 0))
                    if i < NPE - 1:
                        last.then_inc(s_peused, 1)
                filled(last, ("vs", m, 1))
                await_filled(pe, ("vs", m, 1))
                nc.tensor.sem_inc(s_peused, 1)

            for m in range(LT):
                pe.wait_ge(s_h2, m + 1)
                for h in range(2):
                    ps = claim(("h2T", m, h))
                    for k in range(4):
                        last = tr(ps[:, k * P:(k + 1) * P], h2[:, m, (4 * h + k) * P:(4 * h + k + 1) * P], ident[:])
                    filled(last, ("h2T", m, h))
                await_read(pe, ("h2T", m, 1))
                for q4 in range(NQ // 4):
                    ps = claim(("q", m, q4))
                    for i in range(2):
                        n = 2 * q4 + i
                        if m == 0:
                            if n < WRING:
                                w = weights(wq_0 + n)
                            else:
                                pe.wait_ge(s_wq[n - WRING], 16)
                        w = wqs[(wq_0 + n) % WRING if n < WRING else n]
                        for k in range(KD):
                            last = mm(ps[:, i * WCOL:(i + 1) * WCOL], h2Tt[:, k, :], w[:, k, :],
                                      start=(k == 0), stop=(k == KD - 1))
                    filled(last, ("q", m, q4))
                for q4 in range(NQ // 4):
                    ps = claim(("qT", m, q4))
                    await_read(pe, ("q", m, q4))
                    for i in range(4):
                        last = tr(ps[:, i * P:(i + 1) * P], qt[:, q4 % 2, i * P:(i + 1) * P], ident[:])
                    filled(last, ("qT", m, q4))
                    ps = claim(("s", m, q4))
                    await_read(pe, ("qT", m, q4))
                    for i in range(4):
                        last = mm(ps[:, i * P:(i + 1) * P], qTt[:, q4 % 2, i, :], kTt[:, 4 * q4 + i, :],
                                  start=True, stop=True)
                    filled(last, ("s", m, q4))
                if m:
                    add_rows(m - 1)
            add_rows(LT - 1)

        @block.scalar
        def _(act):
            A = nc.scalar.activation
            act.dma_start(xin[:, 0:LT], x[0].rearrange("(m p) d -> p m d", p=P)).then_inc(s_x, 16)
            act.dma_start(xin[:, LT:NT], ctx_in[0].rearrange("(m p) d -> p m d", p=P)).then_inc(s_x, 16)
            act.dma_start(wdt[:], w_in[0][:, O_DT:O_GB].rearrange("(k p) n -> p k n", p=P)).then_inc(s_wdt, 16)
            act.dma_start(dtb[:], dt_bias.rearrange("a d h -> a (d h)").partition_broadcast(P)[:, 0]).then_inc(s_vec, 16)
            act.dma_start(alog[:], a_log.rearrange("a d h -> a (d h)").partition_broadcast(P)[:, 0]).then_inc(s_vec, 16)
            act.dma_start(drow[:], d_skip.partition_broadcast(P)[:, 0]).then_inc(s_vec, 16)

            await_read(act, "rowsA")
            A(cs[:].rearrange("p v k -> p (v k)"), colA[:, A_C:A_C + 2 * KD], ACT.Silu).then_inc(s_cs, 1)
            act.wait_ge(s_x, 32)
            for m in range(NT):
                A(junk[:, m], xin[:, m], ACT.Square, accum_out=ssum[:, m:m + 1]).then_inc(s_ss, 1)
            act.wait_ge(s_ss, NT)
            act.wait_ge(s_dti, 1)
            A(rstd[:], ssum[:], ACT.Sqrt, bias=epsc[:, 0:1], scale=1.0 / D).then_inc(s_sqrt, 1)
            for g in range(4):
                ps = await_bank(act, ("ada1", g))
                release(A(mrow1[0:2, g * 512:(g + 1) * 512], ps[0:2, :], ACT.Copy), ("ada1", g))

            act.wait_ge(s_mod1, 1)
            for m in range(NT):
                v = 0 if m < LT else 1
                ps = await_bank(act, ("hT", m, 0))
                for k in range(4):
                    last = A(hT_tile(m, k), ps[:, k * P:(k + 1) * P], ACT.Identity,
                             bias=mod1[:, k, v:v + 1], scale=mod1[:, KD + k, v:v + 1])
                release(last, ("hT", m, 0))

            for ct in range(NXB):
                await_read(act, ("xl", ct))
                A(xbl[:, ct], xbl[:, ct], ACT.Silu).then_inc(s_xb, 1)
                if ct < NCTX:
                    await_read(act, ("xc", ct))
                    A(xbc_c[:, ct], xbc_c[:, ct], ACT.Silu).then_inc(s_xb, 1)
            for hq in range(4):
                for m in range(LT):
                    ps = await_bank(act, ("z", hq, m))
                    release(A(zs[:, m, hq * WCOL:(hq + 1) * WCOL], ps[:, 0:WCOL], ACT.Silu), ("z", hq, m))

            act.wait_ge(s_dtx, 1)
            A(dte, dta, ACT.Exp).then_inc(s_dte, 1)
            act.wait_ge(s_dtx, 2)
            A(dtl, dtu, ACT.Ln).then_inc(s_dtl, 1)
            act.wait_ge(s_vec, 48)
            A(alog[:], alog[:], ACT.Exp).then_inc(s_dtl, 1)
            for m in range(NT):
                ps = await_bank(act, ("xsT", m, 1))
                release(A(xs[:, m, 512:1024], ps[:, :], ACT.Copy), ("xsT", m, 1))
            for m in range(NT):
                ps = await_bank(act, ("bT", m))
                release(A(Bt[:, m, :], ps[:, :], ACT.Copy), ("bT", m))
            act.wait_ge(s_acs, 1)
            A(eacs[:], acs[:], ACT.Exp).then_inc(s_edec, 1)
            A(edec[:], tot, ACT.Exp).then_inc(s_edec, 1)
            A(wst[:], wst[:], ACT.Exp).then_inc(s_edec, 1)

            for kind, n in SCHED:
                if kind == "proj" and projs[n][0] == "gc":
                    ct = projs[n][1]
                    ps = await_bank(act, ("gc", ct))
                    if ct >= 2:
                        await_read(act, ("v", ct - 2))
                    release(A(gcs[:, ct % 2], ps[:, :], ACT.Copy), ("gc", ct))
                elif kind == "proj" and projs[n][0] == "ada2":
                    g = projs[n][1]
                    ps = await_bank(act, ("ada2", g))
                    if g:
                        await_filled(act, ("ada2T", g - 1))
                    release(A(mrow2[0:2, :], ps[0:2, :], ACT.Copy), ("ada2", g))
                elif kind == "r":
                    m, g = n
                    for d, nm in enumerate(("rf", "rb")):
                        await_read(act, (nm, m, g))
                        buf = mdec[:, (2 * (m * NG + g) + d) % 4]
                        A(buf, buf, ACT.Exp).then_inc(s_dec, 1)

            act.wait_ge(s_y, LT)
            for m in range(LT):
                for g in range(NG):
                    A(xst[:, m % 2, g * GW:(g + 1) * GW] if m < 2 else xdt[:, m % 2, g * GW:(g + 1) * GW],
                      zs[:, m, g * GW:(g + 1) * GW], ACT.Square,
                      accum_out=gss[:, m * NG + g:m * NG + g + 1]).then_inc(s_gss, 1)
            act.wait_ge(s_gss, LT * NG)
            A(grs[:], gss[:], ACT.Sqrt, bias=epsc[:, 0:1], scale=1.0 / GW).then_inc(s_groot, 1)
            await_read(act, "scsum")
            A(scss[:], scss[:], ACT.Sqrt, bias=epsc[:, 0:1], scale=1.0 / D).then_inc(s_scr, 1)
            for r in range(4):
                for h in range(2):
                    ps = await_bank(act, ("row", r, h))
                    release(A(rows[r][:, h * 512:(h + 1) * 512], ps[:, :], ACT.Copy), ("row", r, h))
            for m in range(LT):
                for h in range(2):
                    ps = await_bank(act, ("yT", m, h))
                    for k in range(4):
                        kk = 4 * h + k
                        last = A(yT[:, kk, m * P:(m + 1) * P], ps[:, k * P:(k + 1) * P], ACT.Copy,
                                 scale=colA[:, A_NG + kk:A_NG + kk + 1])
                    release(last, ("yT", m, h))
            act.wait_ge(s_scn, 1)
            def sc_part(tp):
                for nq in range(4):
                    n = 4 * tp + nq
                    ps = await_bank(act, ("wo", nq, 1, tp))
                    if n >= 2:
                        await_read(act, ("wo", (n - 2) % 4, 0, (n - 2) // 4))
                    for i in range(2):
                        m = 2 * tp + i
                        last = A(sBt[:, n % 2, i * WCOL:(i + 1) * WCOL], ps[:, i * WCOL:(i + 1) * WCOL], ACT.Copy,
                                 scale=scss[:, m:m + 1])
                    release(last, ("wo", nq, 1, tp))
                await_read(act, ("wo", 3, 0, tp))

            def norms(tp):
                a, b = 2 * tp, 2 * tp + 2
                for m in range(a, b):
                    A(h2[:, m], mix[m], ACT.Square, accum_out=mss[:, m:m + 1]).then_inc(s_mss, 1)
                act.wait_ge(s_mss, b)
                A(mrs[:, a:b], mss[:, a:b], ACT.Sqrt, bias=epsc[:, 0:1], scale=1.0 / D).then_inc(s_mr, 1)
                for m in range(a, b):
                    act.wait_ge(s_x1n, m + 1)
                    A(mix[m], x1[:, m], ACT.Square, accum_out=xss[:, m:m + 1]).then_inc(s_xss, 1)
                act.wait_ge(s_xss, b)
                A(xrs[:, a:b], xss[:, a:b], ACT.Sqrt, bias=epsc[:, 0:1], scale=1.0 / D).then_inc(s_xr, 1)

            sc_part(0)
            norms(0)
            sc_part(1)
            for q4 in range(NQ // 4):
                ps = await_bank(act, ("kT", q4))
                release(A(kTt[:, 4 * q4:4 * q4 + 4, :].rearrange("p a b -> p (a b)"), ps[:, :], ACT.Copy),
                        ("kT", q4))

            def queries(m):
                if m:
                    await_filled(act, ("q", m - 1, 3))
                for h in range(2):
                    ps = await_bank(act, ("h2T", m, h))
                    release(A(h2Tt[:, 4 * h:4 * h + 4, :].rearrange("p k t -> p (k t)"), ps[:, :], ACT.Copy),
                            ("h2T", m, h))
                if m == 0:
                    norms(1)

                def copy_q(q4):
                    ps = await_bank(act, ("q", m, q4))
                    if q4 >= 2:
                        await_filled(act, ("qT", m, q4 - 2))
                    elif m:
                        await_filled(act, ("qT", m - 1, q4 + 2))
                    release(A(qt[:, q4 % 2], ps[:, :], ACT.Copy), ("q", m, q4))

                copy_q(0)
                copy_q(1)
                for q4 in range(4):
                    ps = await_bank(act, ("qT", m, q4))
                    if q4 >= 2:
                        await_filled(act, ("s", m, q4 - 2))
                    elif m:
                        await_filled(act, ("s", m - 1, q4 + 2))
                    release(A(qTt[:, q4 % 2].rearrange("p i t -> p (i t)"), ps[:, :], ACT.Copy), ("qT", m, q4))
                    if q4 < 2:
                        copy_q(q4 + 2)
                    ps = await_bank(act, ("s", m, q4))
                    if m == 1:
                        act.wait_ge(s_eid, 2 * q4 + 2)
                    elif m and q4 == 0:
                        act.wait_ge(s_pick, m)
                    release(A(scur[:, 4 * q4:4 * q4 + 4, :].rearrange("p i n -> p (i n)"), ps[:, :], ACT.Copy),
                            ("s", m, q4))
                    await_read(act, ("s", m, q4))
                    nc.scalar.sem_inc(s_scur, 1)

            def gates(m):
                act.wait_ge(s_cv, m + 1)
                A(gaten, gaten, ACT.Exp).then_inc(s_ge, 1)

            queries(0)
            queries(1)
            gates(0)
            for m in range(LT):
                act.wait_ge(s_used, m * NDVE + NE)
                A(wexp, dots, ACT.Gelu_apprx_tanh).then_inc(s_gelu, 1)
                act.wait_ge(s_wexp, m + 1)
                for i in range(NPE):
                    if m * NPE + i >= NDG:
                        act.wait_ge(s_peused, m * NPE + i - NDG + 1)
                    A(diag[:, i % NDG], ident[:], ACT.Copy, scale=wexp[:, 2 * i + 1:2 * i + 2]).then_inc(s_diag, 1)
                if m + 1 < LT:
                    gates(m + 1)
                act.wait_ge(s_fss, m + 1)
                A(frs[:], fss[:], ACT.Sqrt, bias=epsc[:, 0:1], scale=1.0 / D).then_inc(s_froot, 1)
                act.wait_ge(s_fin, m + 1)
                act.dma_start(out[0, m * P:(m + 1) * P, :], vacc[:, 0]).then_inc(s_out, 16)
                if m + 2 < LT:
                    queries(m + 2)
                act.wait_ge(s_out, 16 * (m + 1))

        @block.vector
        def _(dve):
            V = nc.vector
            count, base = [0], [0]

            def post(ins):
                count[0] += 1
                ins.then_inc(s_dve, 1)

            def settle(back=0):
                dve.wait_ge(s_dve, base[0] + count[0] - back)

            def link(ins):
                post(ins)
                settle()

            def read_link(ins, name):
                release(ins, name)
                await_read(dve, name)

            V.memset(epsc[:], EPS).then_inc(s_dti, 1)
            ps = await_bank(dve, "rowsA")
            release(V.tensor_copy(colA[:], ps[:, 0:P]), "rowsA")
            ps = await_bank(dve, "rowsB")
            read_link(V.tensor_copy(colB[:, 0:nB], ps[:, 0:nB]), "rowsB")

            dve.wait_ge(s_sqrt, 1)
            link(V.reciprocal(rstd[:], rstd[:]))
            for m in range(NT):
                V.tensor_scalar(xin[:, m], xin[:, m], rstd[:, m:m + 1], None, ALU.mult).then_inc(s_xn, 1)

            ps = await_bank(dve, "ada1T")
            read_link(V.tensor_tensor(mod1[:], ps[:, 0:4 * KD].rearrange("p (j v) -> p j v", v=2),
                                      colB[:, B_BA:B_BA + 2 * KD].unsqueeze(2).to_broadcast([P, 2 * KD, 2]),
                                      ALU.add), "ada1T")
            link(V.tensor_scalar(mod1[:, KD:], mod1[:, KD:], 1.0, None, ALU.add))
            V.tensor_tensor(mod1[:, KD:], mod1[:, KD:],
                            colB[:, B_GPM:B_GPM + KD].unsqueeze(2).to_broadcast([P, KD, 2]),
                            ALU.mult).then_inc(s_mod1, 1)
            dve.wait_ge(s_mod1, 1)
            for m in range(NT):
                v = 0 if m < LT else 1
                ps = await_bank(dve, ("hT", m, 1))
                for k in range(4):
                    last = V.tensor_scalar(hT_tile(m, 4 + k), ps[:, k * P:(k + 1) * P],
                                           mod1[:, KD + 4 + k, v:v + 1], mod1[:, 4 + k, v:v + 1], ALU.mult, ALU.add)
                release(last, ("hT", m, 1))

            def rows_of(ap, width):
                return ap.rearrange("p (r w) -> p r w", w=width)

            def tap(dst, src, k, taps, w):
                o = k - taps // 2
                n = dst.shape[-1]
                d = dst[:, :, max(0, -o):n - max(0, o)]
                s = src[:, :, max(0, o):n + min(0, o)]
                return V.scalar_tensor_tensor(out=d, in0=s, scalar=w, in1=d, op0=ALU.mult, op1=ALU.add)

            for ct in range(NXB):
                sides = [(("xl", ct), xbl[:, ct], SEQ, GRID)]
                if ct < NCTX:
                    sides.append((("xc", ct), xbc_c[:, ct], CTX, CTX))
                views = []
                for name, dst, n, wd in sides:
                    ps = await_bank(dve, name)
                    views.append((name, rows_of(dst, wd), rows_of(ps[:, 0:n], wd)))
                for name, d, s in views:
                    post(V.tensor_scalar(d, s, colA[:, A_CW + 2 * NXB + ct:A_CW + 2 * NXB + ct + 1],
                                         colA[:, A_CB + ct:A_CB + ct + 1], ALU.mult, ALU.add))
                for k in (0, 1, 3, 4):
                    for i, (name, d, s) in enumerate(views):
                        settle(len(views) - 1 - (i if k == 4 else 0))
                        w = colA[:, A_CW + k * NXB + ct:A_CW + k * NXB + ct + 1]
                        if k == 4:
                            release(tap(d, s, k, CONV_K, w), name)
                        else:
                            post(tap(d, s, k, CONV_K, w))

            dve.wait_ge(s_vec, 48)
            ps = await_bank(dve, "dt")
            read_link(V.tensor_tensor(dtx, ps[:, 0:NT * 2 * HEADS].rearrange("p (m d h) -> p d m h", m=NT, d=2),
                                 dtb[:].rearrange("p (d h) -> p d h", d=2).unsqueeze(2).to_broadcast(SM), ALU.add),
                      "dt")
            link(V.tensor_scalar(dta, dtx, -1.0, None, ALU.mult))
            link(V.tensor_tensor(dta, dta, dtx, ALU.min))
            V.sem_inc(s_dtx, 1)
            dve.wait_ge(s_dte, 1)
            link(V.tensor_scalar(dtu, dte, 1.0, None, ALU.add))
            V.sem_inc(s_dtx, 1)
            post(V.tensor_scalar(dts[:], dtu, -1.0, None, ALU.add))
            post(V.tensor_scalar(dtx, dtx, 0.0, None, ALU.max))
            settle()
            link(V.tensor_tensor(dts[:], dte, dts[:], ALU.subtract))
            dve.wait_ge(s_dtl, 2)
            link(V.reciprocal(dte, dtu))
            link(V.tensor_tensor(dts[:], dts[:], dte, ALU.mult))
            link(V.tensor_tensor(dts[:], dts[:], dtl, ALU.add))
            link(V.tensor_tensor(dts[:], dts[:], dtx, ALU.add))
            link(V.tensor_scalar(alog[:], alog[:], -1.0, None, ALU.mult))
            link(V.tensor_tensor(adec[:], dts[:], alog[:].rearrange("p (d h) -> p d h", d=2).unsqueeze(2)
                                 .to_broadcast(SM), ALU.mult))
            V.sem_inc(s_a, 1)
            for m in range(NT):
                ps = await_bank(dve, ("xsT", m, 0))
                release(V.tensor_copy(xs[:, m, 0:512], ps[:, :]), ("xsT", m, 0))
            ps = await_bank(dve, "acs")
            NA = NT * HEADS
            flat = "p d m h -> p (d m h)"
            post(V.tensor_copy(acs[:].rearrange(flat), ps[:, 0:2 * NA]))
            read_link(V.tensor_copy(tot.rearrange(flat), ps[:, 2 * NA:4 * NA]), "acs")
            link(V.tensor_tensor(wst[:], tot, acs[:], ALU.subtract))
            V.sem_inc(s_acs, 1)
            dve.wait_ge(s_edec, 3)
            link(V.tensor_tensor(wst[:], wst[:], dts[:], ALU.mult))
            await_read(dve, ("xsT", NT - 1, 1))
            await_read(dve, ("xsT", NT - 1, 0))

            def heads(ap):
                return ap.rearrange("p (h d) -> p h d", d=HD)

            def per_head(ap, n=HEADS):
                return ap.unsqueeze(2).to_broadcast([P, n, HD])

            def scaled_x(k):
                d, m = steps[k]
                if k >= 2:
                    await_filled(dve, ("st", k - 2, 1))
                V.tensor_tensor(heads(xst[:, k % 2]), heads(xs[:, m]), per_head(wst[:, int(d == "b"), m, :]),
                                ALU.mult).then_inc(s_xst, 1)

            def step(k):
                d, m = steps[k]
                di = int(d == "b")
                hs = hf if d == "f" else hb
                order = [s[1] for s in steps if s[0] == d]
                i = order.index(m)
                slots = [1, 0, 1, 2, 3] if d == "f" else [2, 3, 2, 1, 0]
                dst = slots[i]
                for h in range(2):
                    ps = await_bank(dve, ("st", k, h))
                    cols = slice(h * 512, (h + 1) * 512)
                    if i == 0:
                        read_link(V.tensor_copy(hs[:, dst, cols], ps[:, :]), ("st", k, h))
                    else:
                        src = slots[i - 1]
                        link(V.tensor_tensor(heads(hs[:, dst, cols]), heads(hs[:, src, cols]),
                                             per_head(edec[:, di, m, 8 * h:8 * h + 8], 8), ALU.mult))
                        read_link(V.tensor_tensor(hs[:, dst, cols], hs[:, dst, cols], ps[:, :], ALU.add),
                                  ("st", k, h))

            wcol = lambda ct, k: colB[:, B_SW + k * NX + ct:B_SW + k * NX + ct + 1]

            def proj(n):
                kind, ct = projs[n]
                b = ct % 2
                d, s = rows_of(cv[:, b], GRID), rows_of(gcv[:, b], GRID)
                if kind == "v":
                    await_read(dve, ("gc", ct))
                    ps = await_bank(dve, ("v", ct))
                    read_link(V.tensor_tensor(gcv[:, b], gcs[:, b], ps[:, :], ALU.mult), ("v", ct))
                    link(V.tensor_scalar(d, s, wcol(ct, 1), None, ALU.mult))
                    link(tap(d, s, 0, SC_K, wcol(ct, 0)))
                    link(tap(d, s, 2, SC_K, wcol(ct, 2)))
                elif kind == "gb":
                    ps = await_bank(dve, ("gb", ct))
                    release(V.tensor_tensor(scT[:, ct], cv[:, b], ps[:, :], ALU.mult), ("gb", ct))

            def ada_T(g):
                ps = await_bank(dve, ("ada2T", g))
                j = B_BA + 2 * KD + 4 * g
                release(V.tensor_tensor(modr[:, 4 * g:4 * g + 4], ps[:, 0:8].rearrange("p (j v) -> p j v", v=2)[:, :, 0],
                                        colB[:, j:j + 4], ALU.add), ("ada2T", g))

            def c_times_b(m):
                if m >= 1:
                    await_filled(dve, ("y", m - 1, 1))
                for d in range(2):
                    V.tensor_tensor(heads(xdt[:, d]), heads(xs[:, m]), per_head(dts[:, d, m, :]), ALU.mult) \
                        .then_inc(s_xdt, 1)
                cb = await_bank(dve, ("cb", m)).rearrange("p (g l) -> p g l", g=NG)
                tri_g = lambda tri: tri[:].unsqueeze(1).to_broadcast([P, NG, P])
                post(V.tensor_tensor(cbm[:, 0], cb, tri_g(upper), ALU.mult))
                read_link(V.tensor_tensor(cbm[:, 1], cb, tri_g(lower), ALU.mult), ("cb", m))

            def decay_sums(mg):
                m, g = mg
                b = m * NG + g
                if b >= 2:
                    f = b - 2
                    if f % 2:
                        await_filled(dve, ("y", f // NG, (f % NG) // 2))
                    else:
                        dve.wait_ge(s_mu, f // 2 + 1)
                for d, nm in enumerate(("rf", "rb")):
                    ps = await_bank(dve, (nm, m, g))
                    buf = mdec[:, (2 * b + d) % 4]
                    for r in range(HPG):
                        h = g * HPG + r
                        last = V.tensor_scalar(buf[:, r * P:(r + 1) * P], ps[:, r * P:(r + 1) * P],
                                               acs[:, d, m, h:h + 1], 0.0, ALU.subtract, ALU.min)
                    release(last, (nm, m, g))

            def decay_matrix(mg):
                m, g = mg
                b = m * NG + g
                for d in range(2):
                    buf = mdec[:, (2 * b + d) % 4].rearrange("p (r l) -> p r l", l=P)
                    dve.wait_ge(s_dec, 2 * b + d + 1)
                    V.tensor_tensor(buf, buf, cbm[:, d, g].unsqueeze(1).to_broadcast([P, HPG, P]),
                                    ALU.mult).then_inc(s_m, 1)

            def diagonal_part(mh):
                m, h = mh
                cols = slice(h * 512, (h + 1) * 512)
                link(V.tensor_tensor(heads(yacc[:, cols]), heads(xs[:, m, cols]),
                                     per_head(drow[:, 8 * h:8 * h + 8], 8), ALU.mult))
                ps = await_bank(dve, ("y", m, h))
                read_link(V.tensor_tensor(yacc[:, cols], yacc[:, cols], ps[:, :], ALU.add), ("y", m, h))

            def output(m):
                for di, nm in enumerate(("of", "ob")):
                    for h in range(2):
                        cols = slice(h * 512, (h + 1) * 512)
                        ps = await_bank(dve, (nm, m, h))
                        read_link(V.tensor_tensor(heads(yoff[:, cols]), heads(ps[:, :]),
                                                  per_head(eacs[:, di, m, 8 * h:8 * h + 8], 8), ALU.mult),
                                  (nm, m, h))
                        link(V.tensor_tensor(yacc[:, cols], yacc[:, cols], yoff[:, cols], ALU.add))
                V.tensor_tensor(zs[:, m], zs[:, m], yacc, ALU.mult).then_inc(s_y, 1)
                dve.wait_ge(s_y, m + 1)

            await_read(dve, ("z", 3, LT - 1))
            parts = {"proj": proj, "adaT": ada_T, "x": scaled_x, "step": step, "cb": c_times_b,
                     "r": decay_sums, "m": decay_matrix, "diag": diagonal_part, "out": output}
            for kind, n in SCHED:
                if kind in parts:
                    parts[kind](n)

            dve.wait_ge(s_groot, 1)
            link(V.reciprocal(grs[:], grs[:]))
            for m in range(LT):
                V.tensor_tensor(zs[:, m].rearrange("p (g w) -> p g w", g=NG),
                                zs[:, m].rearrange("p (g w) -> p g w", g=NG),
                                grs[:, m * NG:(m + 1) * NG].unsqueeze(2).to_broadcast([P, NG, GW]),
                                ALU.mult).then_inc(s_yn, 1)
            ps = await_bank(dve, "scsum")
            release(V.tensor_copy(scss[:], ps[:, 0:LT]), "scsum")
            dve.wait_ge(s_scr, 1)
            link(V.reciprocal(scss[:], scss[:]))
            for ct in range(NX):
                last = V.tensor_scalar(scT[:, ct], scT[:, ct], colA[:, A_SG + ct:A_SG + ct + 1], None, ALU.mult)
            last.then_inc(s_scn, 1)

            link(V.tensor_scalar(modr[:, 2 * KD:3 * KD], modr[:, 2 * KD:3 * KD], 1.0, None, ALU.add))
            post(V.tensor_tensor(mod2[:, 0:KD], modr[:, 0:KD], colB[:, B_GQM:B_GQM + KD], ALU.mult))
            post(V.tensor_tensor(mod2[:, KD:2 * KD], modr[:, 3 * KD:4 * KD], colB[:, B_GQF:B_GQF + KD], ALU.mult))
            post(V.tensor_tensor(mod2[:, 2 * KD:3 * KD], modr[:, 2 * KD:3 * KD], colB[:, B_GPF:B_GPF + KD], ALU.mult))
            V.tensor_copy(mod2[:, 3 * KD:4 * KD], modr[:, KD:2 * KD]).then_inc(s_mod2, 1)

            for tp in range(2):
                for nq in range(4):
                    ps = await_bank(dve, ("wo", nq, 0, tp))
                    await_read(dve, ("wo", nq, 1, tp))
                    for i in range(2):
                        m = 2 * tp + i
                        last = V.tensor_tensor(mix[m][:, nq * WCOL:(nq + 1) * WCOL],
                                               ps[:, i * WCOL:(i + 1) * WCOL],
                                               sBt[:, nq % 2, i * WCOL:(i + 1) * WCOL], ALU.add)
                    release(last, ("wo", nq, 0, tp))
                await_read(dve, ("wo", 3, 0, tp))

                dve.wait_ge(s_mr, tp + 1)
                await_read(dve, ("row", 3, 1))
                dve.wait_ge(s_x1, 16)
                a, b = 2 * tp, 2 * tp + 2
                link(V.reciprocal(mrs[:, a:b], mrs[:, a:b]))
                for m in range(a, b):
                    link(V.scalar_tensor_tensor(out=mix[m], in0=mix[m], scalar=mrs[:, m:m + 1],
                                                in1=rows[ROW_GT1], op0=ALU.mult, op1=ALU.mult))
                    V.tensor_tensor(x1[:, m], x1[:, m], mix[m], ALU.add).then_inc(s_x1n, 1)
                dve.wait_ge(s_xr, tp + 1)
                link(V.reciprocal(xrs[:, a:b], xrs[:, a:b]))
                for m in range(a, b):
                    link(V.scalar_tensor_tensor(out=h2[:, m], in0=x1[:, m], scalar=xrs[:, m:m + 1],
                                                in1=rows[ROW_SC2], op0=ALU.mult, op1=ALU.mult))
                    V.tensor_tensor(h2[:, m], h2[:, m], rows[ROW_SH2], ALU.add).then_inc(s_h2, 1)
            def top16(vals, out_v, out_i, lists):
                back = len(lists) - 1
                V.sem_inc(s_gate, 1)
                for j in lists:
                    post(V.max(out_v[:, j, 0:8], vals[:, j]))
                for j in lists:
                    settle(back)
                    V.sem_inc(s_gate, 1)
                    post(V.max_index(out_i[:, j, 0:8], out_v[:, j, 0:8], vals[:, j]))
                for j in lists:
                    settle(back)
                    V.sem_inc(s_gate, 1)
                    post(V.match_replace(vals[:, j], out_v[:, j, 0:8], vals[:, j], TINY))
                for j in lists:
                    settle(back)
                    V.sem_inc(s_gate, 1)
                    post(V.max(out_v[:, j, 8:16], vals[:, j]))
                for j in lists:
                    settle(back)
                    V.sem_inc(s_gate, 1)
                    post(V.max_index(out_i[:, j, 8:16], out_v[:, j, 8:16], vals[:, j]))
                settle()

            sq2 = [P, TOP, TOP]
            jrow = iota_j[:].unsqueeze(1).to_broadcast(sq2)

            def pick_head(h):
                top16(scur, sv, si, (2 * h, 2 * h + 1))
                c3 = cand[:, h].rearrange("p (a b) -> p a b", a=TOP)
                link(V.tensor_tensor(c3, sv[:, 2 * h].unsqueeze(2).to_broadcast(sq2),
                                     sv[:, 2 * h + 1].unsqueeze(1).to_broadcast(sq2), ALU.add))
                top16(cand, cva, cia, (h,))
                post(V.tensor_scalar(ka[:, h], cia[:, h], 4, None, ALU.logical_shift_right))
                post(V.tensor_scalar(kb[:, h], cia[:, h], TOP - 1, None, ALU.bitwise_and))
                settle(1)
                post(V.tensor_tensor(oh1, ka[:, h].unsqueeze(2).to_broadcast(sq2), jrow, ALU.is_equal))
                settle(1)
                post(V.tensor_tensor(oh2, kb[:, h].unsqueeze(2).to_broadcast(sq2), jrow, ALU.is_equal))
                settle(1)
                post(V.tensor_tensor(oh1, oh1, si[:, 2 * h].unsqueeze(1).to_broadcast(sq2), ALU.mult))
                settle(1)
                post(V.tensor_tensor(oh2, oh2, si[:, 2 * h + 1].unsqueeze(1).to_broadcast(sq2), ALU.mult))
                settle(1)
                post(V.tensor_reduce(e1[:, h], oh1, AX, ALU.add))
                settle(1)
                post(V.tensor_reduce(e2[:, h], oh2, AX, ALU.add))
                settle()

            def head_ids(h):
                link(V.scalar_tensor_tensor(out=e1[:, h], in0=e1[:, h], scalar=float(NKEYS), in1=e2[:, h],
                                            op0=ALU.mult, op1=ALU.add))
                V.tensor_copy(eid[:, h * TOP:(h + 1) * TOP], e1[:, h]).then_inc(s_eid, 1)

            def pick_end(t, first=False):
                V.tensor_tensor(gaten, cva, cva[:, :, 0:1].to_broadcast([P, PH, TOP]),
                                ALU.subtract).then_inc(s_cv, 1)
                if not first:
                    link(V.scalar_tensor_tensor(out=e1, in0=e1, scalar=float(NKEYS), in1=e2,
                                                op0=ALU.mult, op1=ALU.add))
                    post(V.tensor_copy(eidn, e1.rearrange("p h k -> p (h k)")))
                dve.wait_ge(s_ge, t + 1)
                link(V.tensor_reduce(gsum, gaten, AX, ALU.add))
                link(V.reciprocal(ginv, gsum))
                V.tensor_tensor(gaten, gaten, ginv.unsqueeze(2).to_broadcast([P, PH, TOP]),
                                ALU.mult).then_inc(s_pick, 1)
                dve.wait_ge(s_pick, t + 1)

            def add_sum(t, h):
                cols = slice(h * 512, (h + 1) * 512)
                if isinstance(t, int):
                    u, more = unit["vs", t, h], 0
                else:
                    u, more = unit["vs", 1, h], t * 2 - 2
                    assert unit["vs", 2, h] == u + 2 * NBANK
                dve.wait_ge(full[u % NBANK], more + (u // NBANK + 1))
                V.tensor_tensor(vacc[:, 0, cols], vacc[:, 0, cols], bank[u % NBANK][:, :],
                                ALU.add).then_inc(free[u % NBANK], 1)
                dve.wait_ge(free[u % NBANK], more + (u // NBANK + 1))

            def dot(t, k):
                s = k % NGS
                dve.wait_ge(s_gsl[s], t * (2 * NE // NGS * 16) + 16 * (k // NGS + 1))
                V.tensor_tensor_reduce(gslot[s], gslot[s], h2c, 1.0, 0.0, ALU.mult, ALU.add,
                                       dots[:, k:k + 1]).then_inc(s_used, 1)

            def tokens_of(t):
                return h2[:, bass.ds(t, 1), :].rearrange("p a d -> p (a d)")

            def first_dots():
                link(V.tensor_copy(h2c, tokens_of(0)))
                for h in range(PH + 1):
                    if h < PH:
                        dve.wait_ge(s_scur, h // 2 + 1)
                        pick_head(h)
                        head_ids(h)
                    if h:
                        for k in range((h - 1) * TOP, h * TOP):
                            dot(0, k)
                pick_end(0, True)
                link(V.tensor_copy(gate, gaten.rearrange("p h k -> p (h k)")))

            def later_dots(t, more):
                post(V.tensor_copy(gate, gaten.rearrange("p h k -> p (h k)")))
                link(V.tensor_copy(h2c, tokens_of(t)))
                for k in range(NE):
                    if more and k == NE // 2:
                        dve.wait_ge(s_scur, t * 4 + 8)
                        pick_head(0)
                    if more and k == NE // 4 * 3:
                        pick_head(1)
                    dot(t, k)

            def weighted_rows(t, more, picks):
                dve.wait_ge(s_gelu, t + 1)
                V.tensor_tensor(wexp, wexp, gate, ALU.mult).then_inc(s_wexp, 1)
                dve.wait_ge(s_wexp, t + 1)
                a = vacc[:, 0]
                for k in range(0, NE, 2):
                    n = NE + k
                    s = n % NGS
                    if more and k in picks:
                        if len(picks) == PH and k == picks[0]:
                            dve.wait_ge(s_scur, 8)
                        pick_head(PH - len(picks) + picks.index(k))
                    if more and k == NE - 4:
                        pick_end(t + 1)
                    dve.wait_ge(s_gsl[s], t * (2 * NE // NGS * 16) + 16 * (n // NGS + 1))
                    if k == 0:
                        V.tensor_scalar(a, gslot[s], wexp[:, k:k + 1], None, ALU.mult).then_inc(s_used, 1)
                    else:
                        dve.wait_ge(s_used, t * NDVE + NE + k // 2)
                        V.scalar_tensor_tensor(out=a, in0=gslot[s], scalar=wexp[:, k:k + 1], in1=a,
                                               op0=ALU.mult, op1=ALU.add).then_inc(s_used, 1)
                if more:
                    dve.wait_ge(s_gsl[NGS - 1], t * (2 * NE // NGS * 16) + 16 * (2 * NE // NGS))
                    V.tensor_copy(eid, eidn).then_inc(s_eid, 1)
                dve.wait_ge(s_used, t * NDVE + NDVE)
                for h in range(2):
                    add_sum(t, h)
                V.tensor_tensor_reduce(vacc[:, 1], vacc[:, 0], vacc[:, 0], 1.0, 0.0, ALU.mult, ALU.add,
                                       fss[:]).then_inc(s_fss, 1)
                dve.wait_ge(s_froot, t + 1)
                link(V.reciprocal(frs[:], frs[:]))
                link(V.scalar_tensor_tensor(out=vacc[:, 0], in0=vacc[:, 0], scalar=frs[:, 0:1],
                                             in1=rows[ROW_GT2], op0=ALU.mult, op1=ALU.mult))
                V.tensor_tensor(vacc[:, 0], vacc[:, 0], x1[:, bass.ds(t, 1), :].rearrange("p a d -> p (a d)"),
                                ALU.add).then_inc(s_fin, 1)

            PICKS_ALL = [n * (NE // 9) for n in range(PH)]
            PICKS = [n * (NE // 8) for n in range(PH - 2)]
            PER_TILE = 5 * (NQ + PH) + 9 * PH + 8
            first_dots()
            weighted_rows(0, True, PICKS_ALL)
            start = count[0]
            count[0] = 0
            with dve.Fori(1, LT - 1) as t:
                base[0] = t * PER_TILE + (start - PER_TILE)
                later_dots(t, True)
                weighted_rows(t, True, PICKS)
                assert count[0] == PER_TILE, count[0]
            base[0] = (LT - 2) * PER_TILE + start
            count[0] = 0
            later_dots(LT - 1, False)
            weighted_rows(LT - 1, False, [])


_INS = ["x", "c", "ctx", "c_ctx", "w_ada", "b_ada", "g_pre_mix", "g_post_mix", "g_pre_ffn", "g_post_ffn",
        "w_in", "ssd_conv_w", "ssd_conv_b", "ssd_dt_bias", "ssd_a_log", "ssd_d", "ssd_norm_g",
        "sc_conv_w", "sc_norm_g", "w_out", "peer_w_q", "peer_keys", "peer_u", "peer_v"]


def kernel(**inputs):
    import numpy as np
    import concourse.bacc as bacc
    from concourse.bass_utils import run_bass_kernel_spmd

    nc = bacc.Bacc("TRN2", target_bir_lowering=False, num_devices=1)
    arrays, args = {}, []
    for name in _INS:
        a = np.ascontiguousarray(inputs[name])
        arrays[f"in_{name}"] = a
        args.append(nc.dram_tensor(f"in_{name}", a.shape, mybir.dt.from_np(a.dtype), kind="ExternalInput").ap())
    out = nc.dram_tensor("out", inputs["x"].shape, F32, kind="ExternalOutput").ap()
    build(nc, *args, out)
    r = run_bass_kernel_spmd(nc, [arrays], core_ids=[0])
    return r.results[0]["out"]
```

```python
from contextlib import ExitStack

import concourse.bass as bass
from concourse import mybir

F32 = mybir.dt.float32
U32 = mybir.dt.uint32
ALU = mybir.AluOpType
ACT = mybir.ActivationFunctionType
AX = mybir.AxisListType.X

P = 128
EPS = 1e-6
KB = 256
CONV_K, SC_K = 5, 3
TOP = 16
NBANK = 8
GRID = 64
TINY = -3.0e38


def build(nc, x, c, ctx_in, c_ctx, w_ada, b_ada, g_pre_mix, g_post_mix, g_pre_ffn, g_post_ffn, w_in,
          conv_w, conv_b, dt_bias, a_log, d_skip, ssd_norm_g, sc_conv_w, sc_norm_g, w_out, w_q, keys,
          u_tab, v_tab, out):
    SEQ, D = x.shape[1], x.shape[2]
    CTX = ctx_in.shape[1]
    KD = D // P
    LT, CT = SEQ // P, CTX // P
    NT = LT + CT
    HEADS = dt_bias.shape[2]
    XBC = conv_w.shape[2]
    NXB = XBC // P
    NX = D // P
    NG = (NXB - NX) // 2
    HPG = HEADS // NG
    HD = D // HEADS
    GW = HPG * HD
    NCTX = NX + NG
    PH, NKEYS = keys.shape[1], keys.shape[3]
    NQ = 2 * PH
    NE = PH * TOP
    O_XBC, O_DT = D, D + XBC
    O_GB = O_DT + 2 * HEADS
    O_GC, O_V = O_GB + D, O_GB + 2 * D
    WCOL = 256
    WRING = 4

    plan = ["rowsA", ("ada1", 0), "rowsB"] + [("ada1", g) for g in range(1, 4)] + ["ada1T"]
    plan += [("hT", m, h) for m in range(NT) for h in range(2)]
    for ct in range(NXB):
        plan.append(("xl", ct))
        if ct < NCTX:
            plan.append(("xc", ct))
        if ct % 2 and ct > 1:
            plan.append(("ada2", ct // 2 - 1))
    plan += ["dt", ("ada2", NXB // 2 - 1)]
    plan += [("z", hq, m) for hq in range(4) for m in range(LT)]
    plan += [("xsT", m, h) for m in range(NT) for h in range(2)] + [("bT", m) for m in range(NT)]
    plan.append("acs")

    fwd = [("f", m) for m in range(LT, NT)] + [("f", m) for m in range(LT - 1)]
    bwd = [("b", m) for m in reversed(range(LT, NT))] + [("b", m) for m in reversed(range(1, LT))]
    steps = [s for pair in zip(fwd, bwd) for s in pair]
    projs = [(kind, ct) for ct in range(NX) for kind in ("gc", "v", "gb")]
    SCHED = [("x", 0), ("x", 1)]
    n_proj = 0

    def add_proj():
        nonlocal n_proj
        if n_proj < len(projs):
            SCHED.append(("proj", n_proj))
            n_proj += 1

    for k in range(len(steps)):
        if k % 2 == 0:
            add_proj()
        SCHED.append(("step", k))
        if k + 2 < len(steps):
            SCHED.append(("x", k + 2))
    for m in range(LT):
        SCHED += [("cb", m), ("r", (m, 0))]
        if m:
            SCHED.append(("out", (m - 1, 1)))
        for g in range(NG):
            SCHED.append(("m", (m, g)))
            add_proj()
            if g == 2:
                SCHED.append(("diag", (m, 0)))
            if g + 1 < NG:
                SCHED.append(("r", (m, g + 1)))
            SCHED.append(("y", (m, g)))
        SCHED += [("off", m), ("diag", (m, 1))]
        add_proj()
        SCHED.append(("out", (m, 0)))
    SCHED.append(("out", (LT - 1, 1)))
    while n_proj < len(projs):
        add_proj()
    for kind, n in SCHED:
        if kind == "proj":
            plan.append(projs[n])
        elif kind == "step":
            plan += [("st", n, 0), ("st", n, 1)]
        elif kind == "cb":
            plan.append(("cb", n))
        elif kind == "r":
            plan.append(("r", *n))
        elif kind == "y" and n[1] % 2 == 0:
            plan.append(("y", n[0], n[1] // 2))
        elif kind == "off":
            plan += [(nm, n, h) for nm in ("of", "ob") for h in range(2)]
    plan.append("scsum")
    plan += [("row", r, h) for r in range(4) for h in range(2)]
    plan += [("yT", m, h) for m in range(LT) for h in range(2)]
    plan += [("wo", nq, part, tp) for tp in range(2) for nq in range(4) for part in range(2)]
    plan += [("kT", q4) for q4 in range(NQ // 4)]
    for m in range(LT):
        plan += [("h2T", m, h) for h in range(2)]
        for q4 in range(NQ // 4):
            plan += [("q", m, q4), ("qT", m, q4), ("s", m, q4)]
        if m:
            plan += [("vs", m - 1, h) for h in range(2)]
    plan += [("vs", LT - 1, h) for h in range(2)]
    unit = {name: n for n, name in enumerate(plan)}
    assert len(unit) == len(plan)

    with ExitStack() as stack:
        def sb(name, shape, dt=F32):
            return stack.enter_context(nc.sbuf_tensor(name, shape, dt))

        def sem(name):
            return stack.enter_context(nc.semaphore(name))

        arena = sb("arena", [P, 196 * KB])

        def at(kib, *dims):
            n = 1
            for d in dims:
                n *= d
            lo = int(kib * KB)
            v = arena[:, lo:lo + n]
            if len(dims) == 1:
                return v
            names = "abcd"[:len(dims)]
            return v.rearrange(f"p ({' '.join(names)}) -> p {' '.join(names)}", **dict(zip(names, dims)))

        wring = at(0, WRING, KD, WCOL)
        hTl, hTc = at(32, KD, SEQ), at(48, KD, CTX)
        xbl = at(56, NXB, SEQ)
        xbc_c = at(88, NCTX, CTX)
        zs = at(100, LT, D)
        scT = at(116, NX, SEQ)
        xin = at(164, NT, D)
        junk = at(56, NT, D)
        Bt = at(152, NT, NG * P)
        xs = at(164, NT, D)
        hf = at(56, LT, D)
        hb = at(132, LT, D)
        gcs, gcv, cv = at(88, 2, SEQ), at(92, 2, SEQ), at(96, 2, SEQ)
        sq, sqacc = at(148, SEQ), at(150, SEQ)
        atri = at(188, 4, HPG * P)
        mrow1 = at(140, 2 * D)
        wada = at(116, 2, KD, WCOL)
        asum = at(152, 2, 2 * WCOL)
        xst = at(188, 2, D)
        after, before = at(184, P), at(184.5, P)
        decay = at(48, 2, HPG * P)
        mdec = at(52, 2, HPG * P)
        yT = at(56, NX, SEQ)
        x1 = at(32, LT, D)
        mixes = at(132, LT, D)
        mix = [mixes[:, (m + 2) % LT] for m in range(LT)]
        sBt = at(152, 2, 512)
        ROW_GT1, ROW_GT2, ROW_SC2, ROW_SH2 = range(4)
        rows = [at(88, D), at(92, D), at(96, D), at(188, D)]
        h2 = at(164, LT, D)
        h2T = at(100, KD, SEQ)
        wqs = [wring[:, n] for n in range(WRING)] + [at(56 + 8 * n, KD, WCOL) for n in range(4)]
        h2Tt = at(142, KD, P)
        kraw = at(180, NQ, P)
        kTt = at(148, NQ, P)
        qt, qTt = at(124, 2, 512), at(128, 2, 4, P)
        scur = at(156, NQ, NKEYS)
        cand = at(132, PH, TOP * TOP)
        oh1, oh2 = at(140, TOP, TOP), at(141, TOP, TOP)
        vacc = at(188, 2, D)
        gslot = [at(100 + 4 * n, D) for n in range(6)] + [at(180 + 4 * n, D) for n in range(2)]
        NGS = len(gslot)
        NPE = NE // 2
        NDVE = NE + NE - NPE
        NDG = 4
        diag = at(146, NDG, P)

        ident, upper, lower, ones = (sb(n, [P, P]) for n in ("ident", "upper", "lower", "ones"))
        colA, colB = sb("colA", [P, P]), sb("colB", [P, P])
        rowA, rowB = at(132, P), at(133, P)
        A_CW, A_CB, A_NG, A_SG, A_C = 0, 80, 96, 104, 112
        B_SW, B_GPM, B_GQM, B_GPF, B_GQF, B_BA = 0, 24, 32, 40, 48, 56
        nB = 104
        cs = sb("cs", [P, 2, KD])
        mod1 = sb("mod1", [P, 2 * KD, 2])
        mod2 = sb("mod2", [P, 4 * KD])
        ssum, rstd = sb("ssum", [P, NT]), sb("rstd", [P, NT])
        wdt = sb("wdt", [P, KD, 2 * HEADS])
        dtb, alog, drow = sb("dtb", [P, 2 * HEADS]), sb("alog", [P, 2 * HEADS]), sb("drow", [P, HEADS])
        SM = [P, 2, NT, HEADS]
        adec, acs = sb("adec", SM), sb("acs", SM)
        dts, eacs, edec, wst = sb("dts", SM), sb("eacs", SM), sb("edec", SM), sb("wst", SM)
        dtx, dta, dte, dtu, dtl, tot = (at(132 + n, 2, NT, HEADS) for n in range(6))
        gss, grs = sb("gss", [P, LT * NG]), sb("grs", [P, LT * NG])
        scss, mss, mrs = sb("scss", [P, LT]), sb("mss", [P, LT]), sb("mrs", [P, LT])
        xss, xrs = sb("xss", [P, LT]), sb("xrs", [P, LT])
        epsc, modr = sb("epsc", [P, 1]), sb("modr", [P, 4 * KD])
        yacc, yoff = at(152, D), at(156, D)
        cbm = at(160, 2, NG, P)
        h2c = at(48, D)
        iota_j, iota_i = sb("iota_j", [P, TOP]), sb("iota_i", [P, TOP], mybir.dt.int32)

        def small(half_kib, *dims, dt=F32):
            v = at(half_kib / 2, *dims)
            return v if dt == F32 else v.bitcast(dt)

        sv, si = small(176, NQ, TOP), small(178, NQ, TOP, dt=U32)
        cva, cia = small(182, PH, TOP), small(183, PH, TOP, dt=U32)
        ka, kb = small(192, PH, TOP, dt=U32), small(193, PH, TOP, dt=U32)
        e1, e2 = small(196, PH, TOP), small(197, PH, TOP)
        eidn, gaten = small(198, PH * TOP, dt=U32), small(199, PH, TOP)
        eid, gate = small(104, PH * TOP, dt=U32), small(105, PH * TOP)
        dots, wexp = small(106, PH * TOP), small(107, PH * TOP)
        gsum, ginv = small(194, PH), small(195, PH)
        fss, frs = sb("fss", [P, 1]), sb("frs", [P, 1])

        bank = [stack.enter_context(nc.psum_tensor(f"bank{i}", [P, 512], F32)) for i in range(NBANK)]
        full = [sem(f"bank{i}_full") for i in range(NBANK)]
        free = [sem(f"bank{i}_free") for i in range(NBANK)]

        s_rowsb = sem("late_vector_rows_loaded")
        s_rows, s_vec, s_x = sem("vector_rows_loaded"), sem("row_vectors_loaded"), sem("tokens_loaded")
        s_w = [sem(f"weights{i}_loaded") for i in range(WRING)]
        s_wused = sem("ada_weights_used")
        s_wq = [sem(f"query_weights{i}_loaded") for i in range(4)]
        s_atri = sem("log_decays_masked")
        s_wdt, s_x1, s_keys = sem("dt_weights_loaded"), sem("tokens_reloaded"), sem("keys_loaded")
        s_cst2, s_const, s_dti = sem("constants_filled"), sem("constants_built"), sem("eps_set")
        s_wada, s_ak, s_asum = [sem(f"modulation_weights{i}_loaded") for i in range(2)], sem("product_added"), sem("products_summed")
        s_cs, s_mod1 = sem("silu_c_ready"), sem("mod1_ready")
        s_ss, s_sqrt, s_xn = sem("squares_summed"), sem("x_root_ready"), sem("x_normed")
        s_xb = sem("xbc_ready")
        s_dtx, s_dte, s_dtl = sem("dt_biased"), sem("dt_exp"), sem("dt_log")
        s_a, s_acs, s_edec = sem("decay_ready"), sem("acs_ready"), sem("decays_exp")
        s_xst, s_tri = sem("xst_ready"), sem("strict_triangles")
        s_sq, s_sqa = sem("sc_squared"), sem("sc_squares_added")
        s_m, s_mu, s_y = sem("mdec_ready"), sem("mdec_used"), sem("y_ready")
        s_gss, s_groot, s_yn = sem("group_squares"), sem("group_root"), sem("y_normed")
        s_scr, s_scn, s_mod2 = sem("sc_root"), sem("sc_normed"), sem("mod2_ready")
        s_mss, s_mr, s_x1n = sem("mix_squares"), sem("mix_root"), sem("x1_ready")
        s_xss, s_xr, s_h2 = sem("x1_squares"), sem("x1_root"), sem("h2_ready")
        s_scur, s_cv, s_ge = sem("scores_staged"), sem("candidates_ranked"), sem("gate_exp")
        s_pick, s_eid = sem("experts_picked"), sem("expert_ids_ready")
        s_gsl = [sem(f"row{i}_landed") for i in range(NGS)]
        s_used, s_gelu = sem("row_used"), sem("gelu_ready")
        s_wexp, s_diag, s_peused = sem("weights_ready"), sem("diagonal_ready"), sem("row_multiplied")
        s_fss, s_froot, s_fin, s_out = sem("out_squares"), sem("out_root"), sem("out_ready"), sem("out_stored")
        s_dve, s_gate, s_pgate = sem("dve_step"), sem("dve_wait_passed"), sem("pool_wait_passed")

        def hT_tile(m, k):
            a, i = (hTl, m) if m < LT else (hTc, m - LT)
            return a[:, k, i * P:(i + 1) * P]

        def bank_of(name):
            return bank[unit[name] % NBANK]

        def claim(name):
            u = unit[name]
            if u >= NBANK:
                nc.tensor.wait_ge(free[u % NBANK], u // NBANK)
            return bank[u % NBANK]

        def filled(ins, name):
            ins.then_inc(full[unit[name] % NBANK], 1)

        def release(ins, name):
            ins.then_inc(free[unit[name] % NBANK], 1)

        def await_read(eng, name):
            u = unit[name]
            eng.wait_ge(free[u % NBANK], u // NBANK + 1)

        def await_filled(eng, name):
            u = unit[name]
            eng.wait_ge(full[u % NBANK], u // NBANK + 1)

        def await_bank(eng, name):
            await_filled(eng, name)
            return bank_of(name)

        loads, users = [], []

        def add_load(w, off, j, user):
            loads.append((w, off, j))
            users.append(user)

        N_ADA1, N_ADA2 = 2 * D // WCOL, 4 * D // WCOL
        for n in range(N_ADA1):
            add_load(w_ada[0], 0, n, ("ada1", n // 2) if n % 2 else n // 2 + 1)
        xbc_0 = len(loads)
        for n in range(XBC // WCOL):
            ct = 2 * n + 1
            add_load(w_in[0], O_XBC, n, ("xc" if ct < NCTX else "xl", ct))
        z_0 = len(loads)
        for n in range(D // WCOL):
            add_load(w_in[0], 0, n, ("z", n, LT - 1))
        proj_load = {}
        for kind, n in projs:
            if n % 2 == 0:
                proj_load[kind, n] = proj_load[kind, n + 1] = len(loads)
                add_load(w_in[0], {"gc": O_GC, "v": O_V, "gb": O_GB}[kind], n // 2, (kind, n + 1))
        wo_0 = len(loads)
        for tp in range(2):
            for n in range(D // WCOL):
                for part in range(2):
                    add_load(w_out[0][part * D:(part + 1) * D], 0, n, ("wo", n, part, tp))
        wq_0 = len(loads)
        for n in range(WRING):
            add_load(w_q[0], 0, n, None)

        block = stack.enter_context(nc.Block())

        @block.sync
        def _(sp):
            rA = [(A_C, c.rearrange("a (c p) -> (a c) p", p=P)),
                  (A_C + KD, c_ctx.rearrange("(c p) -> c p", p=P)),
                  (A_CW, conv_w[0].rearrange("k (c p) -> (k c) p", p=P)),
                  (A_CB, conv_b.rearrange("a (c p) -> (a c) p", p=P)),
                  (A_NG, ssd_norm_g.rearrange("a (c p) -> (a c) p", p=P)),
                  (A_SG, sc_norm_g.rearrange("a (c p) -> (a c) p", p=P))]
            for r, src in rA:
                sp.dma_start(rowA[r:r + src.shape[0], :], src).then_inc(s_rows, 16)
            for n, (w, off, j) in enumerate(loads):
                if 2 <= n < 2 + NT:
                    m = n - 2
                    src = x[0, m * P:(m + 1) * P] if m < LT else ctx_in[0, (m - LT) * P:(m - LT + 1) * P]
                    sp.dma_start(xin[:, m], src).then_inc(s_x, 16)
                if n >= WRING:
                    user = users[n - WRING]
                    if isinstance(user, int):
                        sp.wait_ge(s_wused, user)
                    else:
                        await_filled(sp, user)
                src = w[:, off + j * WCOL:off + (j + 1) * WCOL].rearrange("(k p) n -> p k n", p=P)
                sp.dma_start(wring[:, n % WRING], src).then_inc(s_w[n % WRING], 16)
            await_filled(sp, ("wo", 3, 1, 1))
            for n in range(WRING, 2 * WRING):
                src = w_q[0][:, n * WCOL:(n + 1) * WCOL].rearrange("(k p) n -> p k n", p=P)
                sp.dma_start(wqs[n], src).then_inc(s_wq[n - WRING], 16)

        @block.gpsimd
        def _(pool):
            nc.gpsimd.memset(ident[:], 0.0).then_inc(s_cst2, 1)
            nc.gpsimd.memset(upper[:], 1.0).then_inc(s_cst2, 1)
            nc.gpsimd.memset(lower[:], 1.0).then_inc(s_cst2, 1)
            nc.gpsimd.memset(ones[:], 1.0).then_inc(s_cst2, 1)
            nc.gpsimd.iota(iota_i[:], pattern=[[1, TOP]], base=0, channel_multiplier=0).then_inc(s_cst2, 1)
            pool.wait_ge(s_cst2, 5)
            nc.gpsimd.affine_select(out=ident[:], in_=ident[:], compare_op=ALU.not_equal, fill=1.0, base=0,
                                    pattern=[[-1, P]], channel_multiplier=1).then_inc(s_const, 1)
            nc.gpsimd.affine_select(out=upper[:], in_=upper[:], compare_op=ALU.is_ge, fill=0.0, base=0,
                                    pattern=[[1, P]], channel_multiplier=-1).then_inc(s_const, 1)
            nc.gpsimd.affine_select(out=lower[:], in_=lower[:], compare_op=ALU.is_ge, fill=0.0, base=0,
                                    pattern=[[-1, P]], channel_multiplier=1).then_inc(s_const, 1)
            nc.gpsimd.tensor_copy(iota_j[:], iota_i[:]).then_inc(s_const, 1)
            def load_ada(n):
                src = w_ada[0][:, 2 * D + n * WCOL:2 * D + (n + 1) * WCOL].rearrange("(k p) n -> p k n", p=P)
                pool.dma_start(wada[:, n % 2], src).then_inc(s_wada[n % 2], 16)

            await_filled(pool, ("ada1", 2))
            load_ada(0)
            load_ada(1)
            pool.wait_ge(s_cs, 1)
            for n in range(N_ADA2):
                g, i = n // 2, n % 2
                acc = asum[:, g % 2, i * WCOL:(i + 1) * WCOL]
                if i == 0 and g >= 2:
                    await_filled(pool, ("ada2", g - 2))
                pool.wait_ge(s_wada[i], 16 * (g + 1))
                w = wada[:, i]
                nc.gpsimd.tensor_tensor(w, w, cs[:, 0, :].unsqueeze(2).to_broadcast([P, KD, WCOL]),
                                        ALU.mult).then_inc(s_ak, 1)
                pool.wait_ge(s_ak, 4 * n + 1)
                nc.gpsimd.tensor_tensor(w[:, 0:4], w[:, 0:4], w[:, 4:8], ALU.add).then_inc(s_ak, 1)
                pool.wait_ge(s_ak, 4 * n + 2)
                nc.gpsimd.tensor_tensor(w[:, 0:2], w[:, 0:2], w[:, 2:4], ALU.add).then_inc(s_ak, 1)
                pool.wait_ge(s_ak, 4 * n + 3)
                nc.gpsimd.tensor_tensor(acc, w[:, 0], w[:, 1], ALU.add).then_inc(s_ak, 1)
                pool.wait_ge(s_ak, 4 * n + 4)
                if i:
                    nc.gpsimd.sem_inc(s_asum, 1)
                if n + 2 < N_ADA2:
                    load_ada(n + 2)

            def squares(ct):
                await_read(pool, ("gb", ct))
                if ct == 0:
                    nc.gpsimd.tensor_tensor(sqacc, scT[:, 0], scT[:, 0], ALU.mult).then_inc(s_sqa, 1)
                else:
                    if ct >= 2:
                        pool.wait_ge(s_sqa, ct)
                    nc.gpsimd.tensor_tensor(sq, scT[:, ct], scT[:, ct], ALU.mult).then_inc(s_sq, 1)
                    pool.wait_ge(s_sq, ct)
                    pool.wait_ge(s_sqa, ct)
                    nc.gpsimd.tensor_tensor(sqacc, sqacc, sq, ALU.add).then_inc(s_sqa, 1)

            waiting = None
            for kind, n in SCHED:
                if kind == "r":
                    m, g = n
                    b = m * NG + g
                    if b == 0:
                        await_filled(pool, ("st", len(steps) - 1, 1))
                        nc.gpsimd.tensor_copy(after, lower[:]).then_inc(s_tri, 1)
                        nc.gpsimd.tensor_copy(before, upper[:]).then_inc(s_tri, 1)
                        pool.wait_ge(s_tri, 2)
                        for tri in (after, before):
                            nc.gpsimd.affine_select(out=tri, in_=tri, compare_op=ALU.not_equal, fill=0.0, base=0,
                                                    pattern=[[-1, P]], channel_multiplier=1).then_inc(s_tri, 1)
                    for d, tri in enumerate((upper, lower)):
                        if b >= 2:
                            await_filled(pool, ("r", (b - 2) // NG, (b - 2) % NG))
                        nc.gpsimd.tensor_tensor(
                            atri[:, (2 * b + d) % 4].rearrange("p (r l) -> p r l", l=P),
                            tri[:].unsqueeze(1).to_broadcast([P, HPG, P]),
                            adec[:, d, m, g * HPG:(g + 1) * HPG].unsqueeze(2).to_broadcast([P, HPG, P]),
                            ALU.mult).then_inc(s_atri, 1)
                    if waiting is not None:
                        squares(waiting)
                        waiting = None
                elif kind == "proj" and projs[n][0] == "gb":
                    if waiting is not None:
                        squares(waiting)
                    waiting = projs[n][1]
            if waiting is not None:
                squares(waiting)

            await_filled(pool, ("gb", NX - 1))
            pool.dma_start(x1, x[0].rearrange("(m p) d -> p m d", p=P)).then_inc(s_x1, 16)
            pool.wait_ge(s_gss, LT * NG)
            pool.dma_start(kraw, keys[0].rearrange("h q n d -> n (h q) d")).then_inc(s_keys, 16)


            await_filled(pool, ("wo", 3, 1, 1))
            await_filled(pool, ("kT", NQ // 4 - 1))

            def tile(t, first):
                if not first:
                    pool.wait_ge(s_eid, t + PH)
                    nc.gpsimd.sem_inc(s_pgate, 1)
                for half, tab in enumerate((u_tab[0], v_tab[0])):
                    for k in range(NE):
                        n = half * NE + k
                        if first and n < NE and n % TOP == 0:
                            pool.wait_ge(s_eid, n // TOP + 1)
                            nc.gpsimd.sem_inc(s_pgate, 1)
                        if not (first and n < NGS):
                            o = n - NGS
                            if o < 0 and n % 2:
                                pool.wait_ge(s_peused, t * NPE + (o + 1) // 2)
                            elif o < 0:
                                pool.wait_ge(s_used, t * NDVE + (o + 2) // 2)
                            elif o < NE:
                                pool.wait_ge(s_used, t * NDVE + o + 1)
                            elif o % 2:
                                pool.wait_ge(s_peused, t * NPE + (o - NE) // 2 + 1)
                            else:
                                pool.wait_ge(s_used, t * NDVE + NE + (o - NE) // 2 + 1)
                            nc.gpsimd.sem_inc(s_pgate, 1)
                        nc.gpsimd.indirect_dma_start(
                            gslot[n % NGS], None, tab, bass.IndirectOffsetOnAxis(eid[:, k:k + 1], 0)
                        ).then_inc(s_gsl[n % NGS], 16)

            tile(0, True)
            with pool.Fori(1, LT) as t:
                tile(t, False)

        @block.tensor
        def _(pe):
            mm, tr = nc.tensor.matmul, nc.tensor.transpose

            def weights(n):
                pe.wait_ge(s_w[n % WRING], 16 * (n // WRING + 1))
                return wring[:, n % WRING]

            pe.wait_ge(s_const, 1)
            pe.wait_ge(s_rows, 6 * 16)
            filled(tr(claim("rowsA")[:, 0:P], rowA, ident[:]), "rowsA")

            def ada(name, first, lhs, rows_):
                ps = claim(name)
                for i in range(2):
                    w = weights(first + i)
                    for k in range(KD):
                        last = mm(ps[0:rows_, i * WCOL:(i + 1) * WCOL], lhs(k), w[:, k, :],
                                  start=(k == 0), stop=(k == KD - 1))
                    if i == 0:
                        last.then_inc(s_wused, 1)
                filled(last, name)

            pe.wait_ge(s_cs, 1)
            for g in range(4):
                ada(("ada1", g), 2 * g, lambda k: cs[:, :, k], 2)
                if g == 0:
                    pe.wait_ge(s_rowsb, 6 * 16)
                    filled(tr(claim("rowsB")[:, 0:nB], rowB[0:nB, :], ident[0:nB, 0:nB]), "rowsB")
            ps = claim("ada1T")
            await_read(pe, ("ada1", 3))
            for j in range(2 * KD):
                last = tr(ps[:, 2 * j:2 * j + 2], mrow1[0:2, j * P:(j + 1) * P], ident[0:2, 0:2])
            filled(last, "ada1T")

            for m in range(NT):
                pe.wait_ge(s_xn, m + 1)
                for h in range(2):
                    ps = claim(("hT", m, h))
                    for k in range(4):
                        last = tr(ps[:, k * P:(k + 1) * P], xin[:, m, (4 * h + k) * P:(4 * h + k + 1) * P], ident[:])
                    filled(last, ("hT", m, h))
            await_read(pe, ("hT", NT - 1, 0))
            await_read(pe, ("hT", NT - 1, 1))

            def project_T(name, w, j, hT, n):
                ps = claim(name)
                for k in range(KD):
                    last = mm(ps[:, 0:n], w[:, k, j * P:(j + 1) * P], hT[:, k, :],
                              start=(k == 0), stop=(k == KD - 1))
                filled(last, name)
                return last

            def ada_sum(g):
                ps = claim(("ada2", g))
                pe.wait_ge(s_asum, g + 1)
                for j in range(4):
                    last = mm(ps[:, j:j + 1], asum[:, g % 2, j * P:(j + 1) * P], ones[:, 0:1],
                              start=True, stop=True)
                filled(last, ("ada2", g))

            for n in range(XBC // WCOL):
                w = weights(xbc_0 + n)
                for j in range(2):
                    ct = 2 * n + j
                    project_T(("xl", ct), w, j, hTl, SEQ)
                    if ct < NCTX:
                        project_T(("xc", ct), w, j, hTc, CTX)
                if n:
                    ada_sum(n - 1)

            ps = claim("dt")
            pe.wait_ge(s_wdt, 16)
            for m in range(NT):
                for k in range(KD):
                    last = mm(ps[:, m * 2 * HEADS:(m + 1) * 2 * HEADS], hT_tile(m, k), wdt[:, k, :],
                              start=(k == 0), stop=(k == KD - 1))
            filled(last, "dt")
            ada_sum(NXB // 2 - 1)

            for hq in range(4):
                w = weights(z_0 + hq)
                for m in range(LT):
                    ps = claim(("z", hq, m))
                    for k in range(KD):
                        last = mm(ps[:, 0:WCOL], hT_tile(m, k), w[:, k, :],
                                  start=(k == 0), stop=(k == KD - 1))
                    filled(last, ("z", hq, m))

            pe.wait_ge(s_xb, NXB + NCTX)
            for m in range(NT):
                src, lo = (xbl, m * P) if m < LT else (xbc_c, (m - LT) * P)
                for h in range(2):
                    ps = claim(("xsT", m, h))
                    for k in range(4):
                        last = tr(ps[:, k * P:(k + 1) * P], src[:, 4 * h + k, lo:lo + P], ident[:])
                    filled(last, ("xsT", m, h))
            for m in range(NT):
                src, lo = (xbl, m * P) if m < LT else (xbc_c, (m - LT) * P)
                ps = claim(("bT", m))
                for g in range(NG):
                    last = tr(ps[:, g * P:(g + 1) * P], src[:, NX + g, lo:lo + P], ident[:])
                filled(last, ("bT", m))

            pe.wait_ge(s_a, 1)
            pe.wait_ge(s_const, 4)
            ps = claim("acs")
            NA = NT * HEADS
            ad = adec[:].rearrange("p d m h -> p (d m h)")
            mm(ps[:, 0:NA], upper[:], ad[:, 0:NA], start=True, stop=True)
            mm(ps[:, NA:2 * NA], lower[:], ad[:, NA:2 * NA], start=True, stop=True)
            filled(mm(ps[:, 2 * NA:4 * NA], ones[:], ad, start=True, stop=True), "acs")
            await_read(pe, ("bT", NT - 1))

            def proj(n):
                kind, ct = projs[n]
                project_T((kind, ct), weights(proj_load[kind, ct]), ct % 2, hTl, SEQ)

            def step(k):
                d, m = steps[k]
                pe.wait_ge(s_xst, k + 1)
                for h in range(2):
                    ps = claim(("st", k, h))
                    for g in range(2):
                        gg = 2 * h + g
                        last = mm(ps[:, g * GW:(g + 1) * GW], Bt[:, m, gg * P:(gg + 1) * P],
                                  xst[:, k % 2, gg * GW:(gg + 1) * GW], start=True, stop=True)
                    filled(last, ("st", k, h))

            def c_times_b(m):
                ps = claim(("cb", m))
                for g in range(NG):
                    last = mm(ps[:, g * P:(g + 1) * P], xbl[:, NX + g, m * P:(m + 1) * P],
                              xbl[:, NX + NG + g, m * P:(m + 1) * P], start=True, stop=True)
                filled(last, ("cb", m))

            def decay_sums(mg):
                m, g = mg
                b = m * NG + g
                ps = claim(("r", m, g))
                if b == 0:
                    pe.wait_ge(s_tri, 4)
                for d, tri in enumerate((after, before)):
                    pe.wait_ge(s_atri, 2 * b + d + 1)
                    last = mm(ps[:, :], tri, atri[:, (2 * b + d) % 4], start=(d == 0), stop=(d == 1))
                filled(last, ("r", m, g))

            def diagonal(mg):
                m, g = mg
                b = m * NG + g
                name = ("y", m, g // 2)
                yps = claim(name) if g % 2 == 0 else bank_of(name)
                pe.wait_ge(s_m, b + 1)
                for r in range(HPG):
                    h = g * HPG + r
                    col = (h % 8) * HD
                    last = mm(yps[:, col:col + HD], mdec[:, b % 2, r * P:(r + 1) * P],
                              xs[:, m, h * HD:(h + 1) * HD], start=True, stop=True)
                if g % 2:
                    filled(last, name)
                else:
                    last.then_inc(s_mu, 1)

            def entering(m):
                await_read(pe, ("st", len(steps) - 1, 1))
                for nm, hs in (("of", hf), ("ob", hb)):
                    for h in range(2):
                        ps = claim((nm, m, h))
                        for g in range(2):
                            gg = 2 * h + g
                            last = mm(ps[:, g * GW:(g + 1) * GW], xbl[:, NX + NG + gg, m * P:(m + 1) * P],
                                      hs[:, m, gg * GW:(gg + 1) * GW], start=True, stop=True)
                        filled(last, (nm, m, h))

            parts = {"proj": proj, "step": step, "cb": c_times_b, "r": decay_sums, "y": diagonal, "off": entering}
            for kind, n in SCHED:
                if kind in parts:
                    parts[kind](n)

            ps = claim("scsum")
            pe.wait_ge(s_sqa, NX)
            for m in range(LT):
                last = mm(ps[:, m:m + 1], sqacc[:, m * P:(m + 1) * P], ones[:, 0:1], start=True, stop=True)
            filled(last, "scsum")

            pe.wait_ge(s_mod2, 1)
            for r in range(4):
                for h in range(2):
                    ps = claim(("row", r, h))
                    for k in range(4):
                        j = r * KD + 4 * h + k
                        last = mm(ps[:, k * P:(k + 1) * P], mod2[:, j:j + 1].to_broadcast([P, P]), ident[:],
                                  start=True, stop=True)
                    filled(last, ("row", r, h))

            for m in range(LT):
                pe.wait_ge(s_yn, m + 1)
                for h in range(2):
                    ps = claim(("yT", m, h))
                    for k in range(4):
                        last = tr(ps[:, k * P:(k + 1) * P], zs[:, m, (4 * h + k) * P:(4 * h + k + 1) * P], ident[:])
                    filled(last, ("yT", m, h))
            pe.wait_ge(s_scn, 1)

            for tp in range(2):
                for h in range(2):
                    await_read(pe, ("yT", 2 * tp + 1, h))
                for nq in range(4):
                    for part, src in enumerate((yT, scT)):
                        w = weights(wo_0 + 8 * tp + 2 * nq + part)
                        ps = claim(("wo", nq, part, tp))
                        for i in range(2):
                            m = 2 * tp + i
                            for k in range(KD):
                                last = mm(ps[:, i * WCOL:(i + 1) * WCOL], src[:, k, m * P:(m + 1) * P], w[:, k, :],
                                          start=(k == 0), stop=(k == KD - 1))
                        filled(last, ("wo", nq, part, tp))

            pe.wait_ge(s_keys, 16)
            for q4 in range(NQ // 4):
                ps = claim(("kT", q4))
                for k in range(4):
                    last = tr(ps[:, k * P:(k + 1) * P], kraw[:, 4 * q4 + k, :], ident[:])
                filled(last, ("kT", q4))

            def add_rows(m):
                acc = [claim(("vs", m, h)) for h in range(2)]
                for i in range(NPE):
                    n = NE + 2 * i + 1
                    s = n % NGS
                    pe.wait_ge(s_diag, m * NPE + i + 1)
                    pe.wait_ge(s_gsl[s], 16 * (m * (2 * NE // NGS) + n // NGS + 1))
                    for h in range(2):
                        last = mm(acc[h][:, :], diag[:, i % NDG], gslot[s][:, h * 512:(h + 1) * 512],
                                  start=(i == 0), stop=(i == NPE - 1))
                        if i == NPE - 1 and h == 0:
                            filled(last, ("vs", m, 0))
                    if i < NPE - 1:
                        last.then_inc(s_peused, 1)
                filled(last, ("vs", m, 1))
                await_filled(pe, ("vs", m, 1))
                nc.tensor.sem_inc(s_peused, 1)

            for m in range(LT):
                pe.wait_ge(s_h2, m + 1)
                for h in range(2):
                    ps = claim(("h2T", m, h))
                    for k in range(4):
                        last = tr(ps[:, k * P:(k + 1) * P], h2[:, m, (4 * h + k) * P:(4 * h + k + 1) * P], ident[:])
                    filled(last, ("h2T", m, h))
                await_read(pe, ("h2T", m, 1))
                for q4 in range(NQ // 4):
                    ps = claim(("q", m, q4))
                    for i in range(2):
                        n = 2 * q4 + i
                        if m == 0:
                            if n < WRING:
                                w = weights(wq_0 + n)
                            else:
                                pe.wait_ge(s_wq[n - WRING], 16)
                        w = wqs[(wq_0 + n) % WRING if n < WRING else n]
                        for k in range(KD):
                            last = mm(ps[:, i * WCOL:(i + 1) * WCOL], h2Tt[:, k, :], w[:, k, :],
                                      start=(k == 0), stop=(k == KD - 1))
                    filled(last, ("q", m, q4))
                    ps = claim(("qT", m, q4))
                    await_read(pe, ("q", m, q4))
                    for i in range(4):
                        last = tr(ps[:, i * P:(i + 1) * P], qt[:, q4 % 2, i * P:(i + 1) * P], ident[:])
                    filled(last, ("qT", m, q4))
                    ps = claim(("s", m, q4))
                    await_read(pe, ("qT", m, q4))
                    for i in range(4):
                        last = mm(ps[:, i * P:(i + 1) * P], qTt[:, q4 % 2, i, :], kTt[:, 4 * q4 + i, :],
                                  start=True, stop=True)
                    filled(last, ("s", m, q4))
                if m:
                    add_rows(m - 1)
            add_rows(LT - 1)

        @block.scalar
        def _(act):
            A = nc.scalar.activation
            rB = [(B_SW, sc_conv_w[0].rearrange("k (c p) -> (k c) p", p=P)),
                  (B_GPM, g_pre_mix.rearrange("a (c p) -> (a c) p", p=P)),
                  (B_GQM, g_post_mix.rearrange("a (c p) -> (a c) p", p=P)),
                  (B_GPF, g_pre_ffn.rearrange("a (c p) -> (a c) p", p=P)),
                  (B_GQF, g_post_ffn.rearrange("a (c p) -> (a c) p", p=P)),
                  (B_BA, b_ada.rearrange("a (c p) -> (a c) p", p=P))]
            for r, src in rB:
                act.dma_start(rowB[r:r + src.shape[0], :], src).then_inc(s_rowsb, 16)
            act.dma_start(wdt[:], w_in[0][:, O_DT:O_GB].rearrange("(k p) n -> p k n", p=P)).then_inc(s_wdt, 16)
            act.dma_start(dtb[:], dt_bias.rearrange("a d h -> a (d h)").partition_broadcast(P)[:, 0]).then_inc(s_vec, 16)
            act.dma_start(alog[:], a_log.rearrange("a d h -> a (d h)").partition_broadcast(P)[:, 0]).then_inc(s_vec, 16)
            act.dma_start(drow[:], d_skip.partition_broadcast(P)[:, 0]).then_inc(s_vec, 16)

            await_read(act, "rowsA")
            A(cs[:].rearrange("p v k -> p (v k)"), colA[:, A_C:A_C + 2 * KD], ACT.Silu).then_inc(s_cs, 1)
            act.wait_ge(s_x, NT * 16)
            for m in range(NT):
                A(junk[:, m], xin[:, m], ACT.Square, accum_out=ssum[:, m:m + 1]).then_inc(s_ss, 1)
            act.wait_ge(s_ss, NT)
            act.wait_ge(s_dti, 1)
            A(rstd[:], ssum[:], ACT.Sqrt, bias=epsc[:, 0:1], scale=1.0 / D).then_inc(s_sqrt, 1)
            for g in range(4):
                ps = await_bank(act, ("ada1", g))
                release(A(mrow1[0:2, g * 512:(g + 1) * 512], ps[0:2, :], ACT.Copy), ("ada1", g))

            act.wait_ge(s_mod1, 1)
            for m in range(NT):
                v = 0 if m < LT else 1
                ps = await_bank(act, ("hT", m, 0))
                for k in range(4):
                    last = A(hT_tile(m, k), ps[:, k * P:(k + 1) * P], ACT.Identity,
                             bias=mod1[:, k, v:v + 1], scale=mod1[:, KD + k, v:v + 1])
                release(last, ("hT", m, 0))

            for ct in range(NXB):
                await_read(act, ("xl", ct))
                A(xbl[:, ct], xbl[:, ct], ACT.Silu).then_inc(s_xb, 1)
                if ct < NCTX:
                    await_read(act, ("xc", ct))
                    A(xbc_c[:, ct], xbc_c[:, ct], ACT.Silu).then_inc(s_xb, 1)
            act.wait_ge(s_dtx, 1)
            A(dte, dta, ACT.Exp).then_inc(s_dte, 1)
            act.wait_ge(s_dtx, 2)
            A(dtl, dtu, ACT.Ln).then_inc(s_dtl, 1)
            act.wait_ge(s_vec, 48)
            A(alog[:], alog[:], ACT.Exp).then_inc(s_dtl, 1)
            for hq in range(4):
                for m in range(LT):
                    ps = await_bank(act, ("z", hq, m))
                    release(A(zs[:, m, hq * WCOL:(hq + 1) * WCOL], ps[:, 0:WCOL], ACT.Silu), ("z", hq, m))

            for m in range(NT):
                ps = await_bank(act, ("xsT", m, 1))
                release(A(xs[:, m, 512:1024], ps[:, :], ACT.Copy), ("xsT", m, 1))
            for m in range(NT):
                ps = await_bank(act, ("bT", m))
                release(A(Bt[:, m, :], ps[:, :], ACT.Copy), ("bT", m))
            act.wait_ge(s_acs, 1)
            A(eacs[:], acs[:], ACT.Exp).then_inc(s_edec, 1)
            A(edec[:], tot, ACT.Exp).then_inc(s_edec, 1)
            A(wst[:], wst[:], ACT.Exp).then_inc(s_edec, 1)

            def group_squares(m):
                act.wait_ge(s_y, m + 1)
                for g in range(NG):
                    k = m * NG + g
                    A(xs[:, m, g * GW:(g + 1) * GW], zs[:, m, g * GW:(g + 1) * GW], ACT.Square,
                      accum_out=gss[:, k:k + 1]).then_inc(s_gss, 1)

            for kind, n in SCHED:
                if kind == "proj" and projs[n][0] == "gc":
                    ct = projs[n][1]
                    ps = await_bank(act, ("gc", ct))
                    if ct >= 2:
                        await_read(act, ("v", ct - 2))
                    release(A(gcs[:, ct % 2], ps[:, :], ACT.Copy), ("gc", ct))
                elif kind == "r":
                    m, g = n
                    b = m * NG + g
                    ps = await_bank(act, ("r", m, g))
                    if b >= 2:
                        act.wait_ge(s_m, b - 1)
                    release(A(decay[:, b % 2], ps[:, :], ACT.Exp), ("r", m, g))
                    if g == 1 and m:
                        group_squares(m - 1)

            group_squares(LT - 1)
            act.wait_ge(s_gss, LT * NG)
            A(grs[:], gss[:], ACT.Sqrt, bias=epsc[:, 0:1], scale=1.0 / GW).then_inc(s_groot, 1)
            await_read(act, "scsum")
            A(scss[:], scss[:], ACT.Sqrt, bias=epsc[:, 0:1], scale=1.0 / D).then_inc(s_scr, 1)
            for r in range(4):
                for h in range(2):
                    ps = await_bank(act, ("row", r, h))
                    release(A(rows[r][:, h * 512:(h + 1) * 512], ps[:, :], ACT.Copy), ("row", r, h))
            for m in range(LT):
                ps = await_bank(act, ("yT", m, 0))
                for k in range(4):
                    last = A(yT[:, k, m * P:(m + 1) * P], ps[:, k * P:(k + 1) * P], ACT.Copy,
                             scale=colA[:, A_NG + k:A_NG + k + 1])
                release(last, ("yT", m, 0))
            act.wait_ge(s_scn, 2)
            def sc_part(tp):
                for nq in range(4):
                    n = 4 * tp + nq
                    ps = await_bank(act, ("wo", nq, 1, tp))
                    if n >= 2:
                        await_read(act, ("wo", (n - 2) % 4, 0, (n - 2) // 4))
                    for i in range(2):
                        m = 2 * tp + i
                        last = A(sBt[:, n % 2, i * WCOL:(i + 1) * WCOL], ps[:, i * WCOL:(i + 1) * WCOL], ACT.Copy,
                                 scale=scss[:, m:m + 1])
                    release(last, ("wo", nq, 1, tp))
                await_read(act, ("wo", 3, 0, tp))

            def norms(tp):
                a, b = 2 * tp, 2 * tp + 2
                for m in range(a, b):
                    A(h2[:, m], mix[m], ACT.Square, accum_out=mss[:, m:m + 1]).then_inc(s_mss, 1)
                act.wait_ge(s_mss, b)
                A(mrs[:, a:b], mss[:, a:b], ACT.Sqrt, bias=epsc[:, 0:1], scale=1.0 / D).then_inc(s_mr, 1)
                for m in range(a, b):
                    act.wait_ge(s_x1n, m + 1)
                    A(mix[m], x1[:, m], ACT.Square, accum_out=xss[:, m:m + 1]).then_inc(s_xss, 1)
                act.wait_ge(s_xss, b)
                A(xrs[:, a:b], xss[:, a:b], ACT.Sqrt, bias=epsc[:, 0:1], scale=1.0 / D).then_inc(s_xr, 1)

            sc_part(0)
            norms(0)
            sc_part(1)
            for q4 in range(NQ // 4):
                ps = await_bank(act, ("kT", q4))
                release(A(kTt[:, 4 * q4:4 * q4 + 4, :].rearrange("p a b -> p (a b)"), ps[:, :], ACT.Copy),
                        ("kT", q4))

            def queries(m):
                if m:
                    await_filled(act, ("q", m - 1, 3))
                for h in range(2):
                    ps = await_bank(act, ("h2T", m, h))
                    release(A(h2Tt[:, 4 * h:4 * h + 4, :].rearrange("p k t -> p (k t)"), ps[:, :], ACT.Copy),
                            ("h2T", m, h))
                if m == 0:
                    norms(1)

                def copy_q(q4):
                    ps = await_bank(act, ("q", m, q4))
                    if q4 >= 2:
                        await_filled(act, ("qT", m, q4 - 2))
                    elif m:
                        await_filled(act, ("qT", m - 1, q4 + 2))
                    release(A(qt[:, q4 % 2], ps[:, :], ACT.Copy), ("q", m, q4))

                for q4 in range(4):
                    copy_q(q4)
                    ps = await_bank(act, ("qT", m, q4))
                    if q4 >= 2:
                        await_filled(act, ("s", m, q4 - 2))
                    elif m:
                        await_filled(act, ("s", m - 1, q4 + 2))
                    release(A(qTt[:, q4 % 2].rearrange("p i t -> p (i t)"), ps[:, :], ACT.Copy), ("qT", m, q4))
                    ps = await_bank(act, ("s", m, q4))
                    if m == 1:
                        act.wait_ge(s_eid, 2 * q4 + 2)
                    elif m and q4 == 0:
                        act.wait_ge(s_pick, m)
                    release(A(scur[:, 4 * q4:4 * q4 + 4, :].rearrange("p i n -> p (i n)"), ps[:, :], ACT.Copy),
                            ("s", m, q4))
                    await_read(act, ("s", m, q4))
                    nc.scalar.sem_inc(s_scur, 1)

            def gates(m):
                act.wait_ge(s_cv, m + 1)
                A(gaten, gaten, ACT.Exp).then_inc(s_ge, 1)

            queries(0)
            queries(1)
            gates(0)
            for m in range(LT):
                act.wait_ge(s_used, m * NDVE + NE)
                A(wexp, dots, ACT.Gelu_apprx_tanh).then_inc(s_gelu, 1)
                act.wait_ge(s_wexp, m + 1)
                for i in range(NPE):
                    if m * NPE + i >= NDG:
                        act.wait_ge(s_peused, m * NPE + i - NDG + 1)
                    A(diag[:, i % NDG], ident[:], ACT.Copy, scale=wexp[:, 2 * i + 1:2 * i + 2]).then_inc(s_diag, 1)
                if m + 1 < LT:
                    gates(m + 1)
                act.wait_ge(s_fss, m + 1)
                A(frs[:], fss[:], ACT.Sqrt, bias=epsc[:, 0:1], scale=1.0 / D).then_inc(s_froot, 1)
                act.wait_ge(s_fin, m + 1)
                act.dma_start(out[0, m * P:(m + 1) * P, :], vacc[:, 0]).then_inc(s_out, 16)
                if m + 2 < LT:
                    queries(m + 2)
                act.wait_ge(s_out, 16 * (m + 1))

        @block.vector
        def _(dve):
            V = nc.vector
            count, base = [0], [0]

            def post(ins):
                count[0] += 1
                ins.then_inc(s_dve, 1)

            def settle(back=0):
                dve.wait_ge(s_dve, base[0] + count[0] - back)

            def link(ins):
                post(ins)
                settle()

            def read_link(ins, name):
                release(ins, name)
                await_read(dve, name)

            V.memset(epsc[:], EPS).then_inc(s_dti, 1)
            ps = await_bank(dve, "rowsA")
            release(V.tensor_copy(colA[:], ps[:, 0:P]), "rowsA")
            ps = await_bank(dve, "rowsB")
            read_link(V.tensor_copy(colB[:, 0:nB], ps[:, 0:nB]), "rowsB")

            dve.wait_ge(s_sqrt, 1)
            link(V.reciprocal(rstd[:], rstd[:]))
            for m in range(NT):
                V.tensor_scalar(xin[:, m], xin[:, m], rstd[:, m:m + 1], None, ALU.mult).then_inc(s_xn, 1)

            ps = await_bank(dve, "ada1T")
            read_link(V.tensor_tensor(mod1[:], ps[:, 0:4 * KD].rearrange("p (j v) -> p j v", v=2),
                                      colB[:, B_BA:B_BA + 2 * KD].unsqueeze(2).to_broadcast([P, 2 * KD, 2]),
                                      ALU.add), "ada1T")
            link(V.tensor_scalar(mod1[:, KD:], mod1[:, KD:], 1.0, None, ALU.add))
            V.tensor_tensor(mod1[:, KD:], mod1[:, KD:],
                            colB[:, B_GPM:B_GPM + KD].unsqueeze(2).to_broadcast([P, KD, 2]),
                            ALU.mult).then_inc(s_mod1, 1)
            dve.wait_ge(s_mod1, 1)
            for m in range(NT):
                v = 0 if m < LT else 1
                ps = await_bank(dve, ("hT", m, 1))
                for k in range(4):
                    last = V.tensor_scalar(hT_tile(m, 4 + k), ps[:, k * P:(k + 1) * P],
                                           mod1[:, KD + 4 + k, v:v + 1], mod1[:, 4 + k, v:v + 1], ALU.mult, ALU.add)
                release(last, ("hT", m, 1))

            def rows_of(ap, width):
                return ap.rearrange("p (r w) -> p r w", w=width)

            def tap(dst, src, k, taps, w):
                o = k - taps // 2
                n = dst.shape[-1]
                d = dst[:, :, max(0, -o):n - max(0, o)]
                s = src[:, :, max(0, o):n + min(0, o)]
                return V.scalar_tensor_tensor(out=d, in0=s, scalar=w, in1=d, op0=ALU.mult, op1=ALU.add)

            def ada_piece(g):
                ps = await_bank(dve, ("ada2", g))
                j = B_BA + 2 * KD + 4 * g
                release(V.tensor_tensor(modr[:, 4 * g:4 * g + 4], ps[:, 0:4], colB[:, j:j + 4], ALU.add),
                        ("ada2", g))

            for ct in range(NXB):
                sides = [(("xl", ct), xbl[:, ct], SEQ, GRID)]
                if ct < NCTX:
                    sides.append((("xc", ct), xbc_c[:, ct], CTX, CTX))
                views = []
                for name, dst, n, wd in sides:
                    ps = await_bank(dve, name)
                    views.append((name, rows_of(dst, wd), rows_of(ps[:, 0:n], wd)))
                for name, d, s in views:
                    post(V.tensor_scalar(d, s, colA[:, A_CW + 2 * NXB + ct:A_CW + 2 * NXB + ct + 1],
                                         colA[:, A_CB + ct:A_CB + ct + 1], ALU.mult, ALU.add))
                for k in (0, 1, 3, 4):
                    for i, (name, d, s) in enumerate(views):
                        settle(len(views) - 1 - (i if k == 4 else 0))
                        w = colA[:, A_CW + k * NXB + ct:A_CW + k * NXB + ct + 1]
                        if k == 4:
                            release(tap(d, s, k, CONV_K, w), name)
                        else:
                            post(tap(d, s, k, CONV_K, w))
                if ct % 2 and ct > 1:
                    ada_piece(ct // 2 - 1)

            dve.wait_ge(s_vec, 48)
            ps = await_bank(dve, "dt")
            read_link(V.tensor_tensor(dtx, ps[:, 0:NT * 2 * HEADS].rearrange("p (m d h) -> p d m h", m=NT, d=2),
                                 dtb[:].rearrange("p (d h) -> p d h", d=2).unsqueeze(2).to_broadcast(SM), ALU.add),
                      "dt")
            ada_piece(NXB // 2 - 1)
            await_read(dve, ("ada2", NXB // 2 - 1))
            link(V.tensor_scalar(modr[:, 2 * KD:3 * KD], modr[:, 2 * KD:3 * KD], 1.0, None, ALU.add))
            post(V.tensor_tensor(mod2[:, 0:KD], modr[:, 0:KD], colB[:, B_GQM:B_GQM + KD], ALU.mult))
            post(V.tensor_tensor(mod2[:, KD:2 * KD], modr[:, 3 * KD:4 * KD], colB[:, B_GQF:B_GQF + KD], ALU.mult))
            post(V.tensor_tensor(mod2[:, 2 * KD:3 * KD], modr[:, 2 * KD:3 * KD], colB[:, B_GPF:B_GPF + KD], ALU.mult))
            V.tensor_copy(mod2[:, 3 * KD:4 * KD], modr[:, KD:2 * KD]).then_inc(s_mod2, 1)


            link(V.tensor_scalar(dta, dtx, -1.0, None, ALU.mult))
            link(V.tensor_tensor(dta, dta, dtx, ALU.min))
            V.sem_inc(s_dtx, 1)
            dve.wait_ge(s_dte, 1)
            link(V.tensor_scalar(dtu, dte, 1.0, None, ALU.add))
            V.sem_inc(s_dtx, 1)
            post(V.tensor_scalar(dts[:], dtu, -1.0, None, ALU.add))
            post(V.tensor_scalar(dtx, dtx, 0.0, None, ALU.max))
            settle()
            link(V.tensor_tensor(dts[:], dte, dts[:], ALU.subtract))
            dve.wait_ge(s_dtl, 2)
            link(V.reciprocal(dte, dtu))
            link(V.tensor_tensor(dts[:], dts[:], dte, ALU.mult))
            link(V.tensor_tensor(dts[:], dts[:], dtl, ALU.add))
            link(V.tensor_tensor(dts[:], dts[:], dtx, ALU.add))
            link(V.tensor_scalar(alog[:], alog[:], -1.0, None, ALU.mult))
            link(V.tensor_tensor(adec[:], dts[:], alog[:].rearrange("p (d h) -> p d h", d=2).unsqueeze(2)
                                 .to_broadcast(SM), ALU.mult))
            V.sem_inc(s_a, 1)
            for m in range(NT):
                ps = await_bank(dve, ("xsT", m, 0))
                release(V.tensor_copy(xs[:, m, 0:512], ps[:, :]), ("xsT", m, 0))
            ps = await_bank(dve, "acs")
            NA = NT * HEADS
            flat = "p d m h -> p (d m h)"
            post(V.tensor_copy(acs[:].rearrange(flat), ps[:, 0:2 * NA]))
            read_link(V.tensor_copy(tot.rearrange(flat), ps[:, 2 * NA:4 * NA]), "acs")
            link(V.tensor_tensor(wst[:], tot, acs[:], ALU.subtract))
            V.sem_inc(s_acs, 1)
            dve.wait_ge(s_edec, 3)
            link(V.tensor_tensor(wst[:], wst[:], dts[:], ALU.mult))
            await_read(dve, ("xsT", NT - 1, 1))
            await_read(dve, ("xsT", NT - 1, 0))

            def heads(ap):
                return ap.rearrange("p (h d) -> p h d", d=HD)

            def per_head(ap, n=HEADS):
                return ap.unsqueeze(2).to_broadcast([P, n, HD])

            def scaled_x(k):
                d, m = steps[k]
                if k >= 2:
                    await_filled(dve, ("st", k - 2, 1))
                V.tensor_tensor(heads(xst[:, k % 2]), heads(xs[:, m]), per_head(wst[:, int(d == "b"), m, :]),
                                ALU.mult).then_inc(s_xst, 1)

            def step(k):
                d, m = steps[k]
                di = int(d == "b")
                hs = hf if d == "f" else hb
                order = [s[1] for s in steps if s[0] == d]
                i = order.index(m)
                slots = [1, 0, 1, 2, 3] if d == "f" else [2, 3, 2, 1, 0]
                dst = slots[i]
                for h in range(2):
                    ps = await_bank(dve, ("st", k, h))
                    cols = slice(h * 512, (h + 1) * 512)
                    if i == 0:
                        read_link(V.tensor_copy(hs[:, dst, cols], ps[:, :]), ("st", k, h))
                    else:
                        src = slots[i - 1]
                        link(V.tensor_tensor(heads(hs[:, dst, cols]), heads(hs[:, src, cols]),
                                             per_head(edec[:, di, m, 8 * h:8 * h + 8], 8), ALU.mult))
                        read_link(V.tensor_tensor(hs[:, dst, cols], hs[:, dst, cols], ps[:, :], ALU.add),
                                  ("st", k, h))

            wcol = lambda ct, k: colB[:, B_SW + k * NX + ct:B_SW + k * NX + ct + 1]

            def proj(n):
                kind, ct = projs[n]
                b = ct % 2
                d, s = rows_of(cv[:, b], GRID), rows_of(gcv[:, b], GRID)
                if kind == "v":
                    await_read(dve, ("gc", ct))
                    ps = await_bank(dve, ("v", ct))
                    read_link(V.tensor_tensor(gcv[:, b], gcs[:, b], ps[:, :], ALU.mult), ("v", ct))
                    link(V.tensor_scalar(d, s, wcol(ct, 1), None, ALU.mult))
                    link(tap(d, s, 0, SC_K, wcol(ct, 0)))
                    link(tap(d, s, 2, SC_K, wcol(ct, 2)))
                elif kind == "gb":
                    ps = await_bank(dve, ("gb", ct))
                    release(V.tensor_tensor(scT[:, ct], cv[:, b], ps[:, :], ALU.mult), ("gb", ct))

            def c_times_b(m):
                cb = await_bank(dve, ("cb", m)).rearrange("p (g l) -> p g l", g=NG)
                tri_g = lambda tri: tri[:].unsqueeze(1).to_broadcast([P, NG, P])
                post(V.tensor_tensor(cbm[:, 0], cb, tri_g(upper), ALU.mult))
                read_link(V.tensor_tensor(cbm[:, 1], cb, tri_g(lower), ALU.mult), ("cb", m))

            def dt_times_cb(mg):
                m, g = mg
                b = m * NG + g
                if b >= 2:
                    f = b - 2
                    if f % 2:
                        await_filled(dve, ("y", f // NG, (f % NG) // 2))
                    else:
                        dve.wait_ge(s_mu, f // 2 + 1)
                for r in range(HPG):
                    h = g * HPG + r
                    post(V.tensor_scalar(mdec[:, b % 2, r * P:(r + 1) * P], cbm[:, 0, g],
                                         dts[:, 0, m, h:h + 1], None, ALU.mult))
                for r in range(HPG):
                    h = g * HPG + r
                    buf = mdec[:, b % 2, r * P:(r + 1) * P]
                    settle(HPG - 1)
                    post(V.scalar_tensor_tensor(out=buf, in0=cbm[:, 1, g], scalar=dts[:, 1, m, h:h + 1], in1=buf,
                                                op0=ALU.mult, op1=ALU.add))

            def decay_matrix(mg):
                m, g = mg
                b = m * NG + g
                await_read(dve, ("r", m, g))
                settle()
                V.tensor_tensor(mdec[:, b % 2], mdec[:, b % 2], decay[:, b % 2], ALU.mult).then_inc(s_m, 1)

            def diagonal_part(mh):
                m, h = mh
                cols = slice(h * 512, (h + 1) * 512)
                link(V.tensor_tensor(heads(yacc[:, cols]), heads(xs[:, m, cols]),
                                     per_head(drow[:, 8 * h:8 * h + 8], 8), ALU.mult))
                ps = await_bank(dve, ("y", m, h))
                read_link(V.tensor_tensor(yacc[:, cols], yacc[:, cols], ps[:, :], ALU.add), ("y", m, h))

            def output(md):
                m, di = md
                nm = ("of", "ob")[di]
                for h in range(2):
                    cols = slice(h * 512, (h + 1) * 512)
                    ps = await_bank(dve, (nm, m, h))
                    read_link(V.tensor_tensor(heads(yoff[:, cols]), heads(ps[:, :]),
                                              per_head(eacs[:, di, m, 8 * h:8 * h + 8], 8), ALU.mult),
                              (nm, m, h))
                    link(V.tensor_tensor(yacc[:, cols], yacc[:, cols], yoff[:, cols], ALU.add))
                if di == 0:
                    return
                V.tensor_tensor(zs[:, m], zs[:, m], yacc, ALU.mult).then_inc(s_y, 1)
                dve.wait_ge(s_y, m + 1)

            await_read(dve, ("z", 3, LT - 1))
            parts = {"proj": proj, "x": scaled_x, "step": step, "cb": c_times_b,
                     "r": dt_times_cb, "m": decay_matrix, "diag": diagonal_part, "out": output}
            for kind, n in SCHED:
                if kind in parts:
                    parts[kind](n)

            ps = await_bank(dve, "scsum")
            release(V.tensor_copy(scss[:], ps[:, 0:LT]), "scsum")
            for ct in range(NX):
                last = V.tensor_scalar(scT[:, ct], scT[:, ct], colA[:, A_SG + ct:A_SG + ct + 1], None, ALU.mult)
            last.then_inc(s_scn, 1)

            dve.wait_ge(s_groot, 1)
            link(V.reciprocal(grs[:], grs[:]))
            for m in range(LT):
                V.tensor_tensor(zs[:, m].rearrange("p (g w) -> p g w", g=NG),
                                zs[:, m].rearrange("p (g w) -> p g w", g=NG),
                                grs[:, m * NG:(m + 1) * NG].unsqueeze(2).to_broadcast([P, NG, GW]),
                                ALU.mult).then_inc(s_yn, 1)
            dve.wait_ge(s_scr, 1)
            link(V.reciprocal(scss[:], scss[:]))
            V.sem_inc(s_scn, 1)
            for m in range(LT):
                ps = await_bank(dve, ("yT", m, 1))
                for k in range(4):
                    kk = 4 + k
                    last = V.tensor_scalar(yT[:, kk, m * P:(m + 1) * P], ps[:, k * P:(k + 1) * P],
                                           colA[:, A_NG + kk:A_NG + kk + 1], None, ALU.mult)
                release(last, ("yT", m, 1))

            for tp in range(2):
                for nq in range(4):
                    ps = await_bank(dve, ("wo", nq, 0, tp))
                    await_read(dve, ("wo", nq, 1, tp))
                    for i in range(2):
                        m = 2 * tp + i
                        last = V.tensor_tensor(mix[m][:, nq * WCOL:(nq + 1) * WCOL],
                                               ps[:, i * WCOL:(i + 1) * WCOL],
                                               sBt[:, nq % 2, i * WCOL:(i + 1) * WCOL], ALU.add)
                    release(last, ("wo", nq, 0, tp))
                await_read(dve, ("wo", 3, 0, tp))

                dve.wait_ge(s_mr, tp + 1)
                await_read(dve, ("row", 3, 1))
                dve.wait_ge(s_x1, 16)
                a, b = 2 * tp, 2 * tp + 2
                link(V.reciprocal(mrs[:, a:b], mrs[:, a:b]))
                for m in range(a, b):
                    link(V.scalar_tensor_tensor(out=mix[m], in0=mix[m], scalar=mrs[:, m:m + 1],
                                                in1=rows[ROW_GT1], op0=ALU.mult, op1=ALU.mult))
                    V.tensor_tensor(x1[:, m], x1[:, m], mix[m], ALU.add).then_inc(s_x1n, 1)
                dve.wait_ge(s_xr, tp + 1)
                link(V.reciprocal(xrs[:, a:b], xrs[:, a:b]))
                for m in range(a, b):
                    link(V.scalar_tensor_tensor(out=h2[:, m], in0=x1[:, m], scalar=xrs[:, m:m + 1],
                                                in1=rows[ROW_SC2], op0=ALU.mult, op1=ALU.mult))
                    V.tensor_tensor(h2[:, m], h2[:, m], rows[ROW_SH2], ALU.add).then_inc(s_h2, 1)
            def top16(vals, out_v, out_i, lists):
                back = len(lists) - 1
                V.sem_inc(s_gate, 1)
                for j in lists:
                    post(V.max(out_v[:, j, 0:8], vals[:, j]))
                for j in lists:
                    settle(back)
                    V.sem_inc(s_gate, 1)
                    post(V.max_index(out_i[:, j, 0:8], out_v[:, j, 0:8], vals[:, j]))
                for j in lists:
                    settle(back)
                    V.sem_inc(s_gate, 1)
                    post(V.match_replace(vals[:, j], out_v[:, j, 0:8], vals[:, j], TINY))
                for j in lists:
                    settle(back)
                    V.sem_inc(s_gate, 1)
                    post(V.max(out_v[:, j, 8:16], vals[:, j]))
                for j in lists:
                    settle(back)
                    V.sem_inc(s_gate, 1)
                    post(V.max_index(out_i[:, j, 8:16], out_v[:, j, 8:16], vals[:, j]))
                settle()

            sq2 = [P, TOP, TOP]
            jrow = iota_j[:].unsqueeze(1).to_broadcast(sq2)

            def pick_head(h):
                top16(scur, sv, si, (2 * h, 2 * h + 1))
                c3 = cand[:, h].rearrange("p (a b) -> p a b", a=TOP)
                link(V.tensor_tensor(c3, sv[:, 2 * h].unsqueeze(2).to_broadcast(sq2),
                                     sv[:, 2 * h + 1].unsqueeze(1).to_broadcast(sq2), ALU.add))
                top16(cand, cva, cia, (h,))
                post(V.tensor_scalar(ka[:, h], cia[:, h], 4, None, ALU.logical_shift_right))
                post(V.tensor_scalar(kb[:, h], cia[:, h], TOP - 1, None, ALU.bitwise_and))
                settle(1)
                post(V.tensor_tensor(oh1, ka[:, h].unsqueeze(2).to_broadcast(sq2), jrow, ALU.is_equal))
                settle(1)
                post(V.tensor_tensor(oh2, kb[:, h].unsqueeze(2).to_broadcast(sq2), jrow, ALU.is_equal))
                settle(1)
                post(V.tensor_tensor(oh1, oh1, si[:, 2 * h].unsqueeze(1).to_broadcast(sq2), ALU.mult))
                settle(1)
                post(V.tensor_tensor(oh2, oh2, si[:, 2 * h + 1].unsqueeze(1).to_broadcast(sq2), ALU.mult))
                settle(1)
                post(V.tensor_reduce(e1[:, h], oh1, AX, ALU.add))
                settle(1)
                post(V.tensor_reduce(e2[:, h], oh2, AX, ALU.add))
                settle()

            def head_ids(h):
                link(V.scalar_tensor_tensor(out=e1[:, h], in0=e1[:, h], scalar=float(NKEYS), in1=e2[:, h],
                                            op0=ALU.mult, op1=ALU.add))
                V.tensor_copy(eid[:, h * TOP:(h + 1) * TOP], e1[:, h]).then_inc(s_eid, 1)

            def pick_end(t, first=False):
                V.tensor_tensor(gaten, cva, cva[:, :, 0:1].to_broadcast([P, PH, TOP]),
                                ALU.subtract).then_inc(s_cv, 1)
                if not first:
                    link(V.scalar_tensor_tensor(out=e1, in0=e1, scalar=float(NKEYS), in1=e2,
                                                op0=ALU.mult, op1=ALU.add))
                    post(V.tensor_copy(eidn, e1.rearrange("p h k -> p (h k)")))
                dve.wait_ge(s_ge, t + 1)
                link(V.tensor_reduce(gsum, gaten, AX, ALU.add))
                link(V.reciprocal(ginv, gsum))
                V.tensor_tensor(gaten, gaten, ginv.unsqueeze(2).to_broadcast([P, PH, TOP]),
                                ALU.mult).then_inc(s_pick, 1)
                dve.wait_ge(s_pick, t + 1)

            def add_sum(t, h):
                cols = slice(h * 512, (h + 1) * 512)
                if isinstance(t, int):
                    u, more = unit["vs", t, h], 0
                else:
                    u, more = unit["vs", 1, h], t * 2 - 2
                    assert unit["vs", 2, h] == u + 2 * NBANK
                dve.wait_ge(full[u % NBANK], more + (u // NBANK + 1))
                V.tensor_tensor(vacc[:, 0, cols], vacc[:, 0, cols], bank[u % NBANK][:, :],
                                ALU.add).then_inc(free[u % NBANK], 1)
                dve.wait_ge(free[u % NBANK], more + (u // NBANK + 1))

            def dot(t, k):
                s = k % NGS
                dve.wait_ge(s_gsl[s], t * (2 * NE // NGS * 16) + 16 * (k // NGS + 1))
                V.tensor_tensor_reduce(gslot[s], gslot[s], h2c, 1.0, 0.0, ALU.mult, ALU.add,
                                       dots[:, k:k + 1]).then_inc(s_used, 1)

            def tokens_of(t):
                return h2[:, bass.ds(t, 1), :].rearrange("p a d -> p (a d)")

            def first_dots():
                link(V.tensor_copy(h2c, tokens_of(0)))
                for h in range(PH + 1):
                    if h < PH:
                        dve.wait_ge(s_scur, h // 2 + 1)
                        pick_head(h)
                        head_ids(h)
                    if h:
                        for k in range((h - 1) * TOP, h * TOP):
                            dot(0, k)
                pick_end(0, True)
                link(V.tensor_copy(gate, gaten.rearrange("p h k -> p (h k)")))

            def later_dots(t, more):
                post(V.tensor_copy(gate, gaten.rearrange("p h k -> p (h k)")))
                link(V.tensor_copy(h2c, tokens_of(t)))
                for k in range(NE):
                    if more and k == NE // 2:
                        dve.wait_ge(s_scur, t * 4 + 8)
                        pick_head(0)
                    if more and k == NE // 4 * 3:
                        pick_head(1)
                    dot(t, k)

            def weighted_rows(t, more, picks):
                dve.wait_ge(s_gelu, t + 1)
                V.tensor_tensor(wexp, wexp, gate, ALU.mult).then_inc(s_wexp, 1)
                dve.wait_ge(s_wexp, t + 1)
                a = vacc[:, 0]
                for k in range(0, NE, 2):
                    n = NE + k
                    s = n % NGS
                    if more and k in picks:
                        if len(picks) == PH and k == picks[0]:
                            dve.wait_ge(s_scur, 8)
                        pick_head(PH - len(picks) + picks.index(k))
                    if more and k == NE - 4:
                        pick_end(t + 1)
                    dve.wait_ge(s_gsl[s], t * (2 * NE // NGS * 16) + 16 * (n // NGS + 1))
                    if k == 0:
                        V.tensor_scalar(a, gslot[s], wexp[:, k:k + 1], None, ALU.mult).then_inc(s_used, 1)
                    else:
                        dve.wait_ge(s_used, t * NDVE + NE + k // 2)
                        V.scalar_tensor_tensor(out=a, in0=gslot[s], scalar=wexp[:, k:k + 1], in1=a,
                                               op0=ALU.mult, op1=ALU.add).then_inc(s_used, 1)
                if more:
                    dve.wait_ge(s_gsl[NGS - 1], t * (2 * NE // NGS * 16) + 16 * (2 * NE // NGS))
                    V.tensor_copy(eid, eidn).then_inc(s_eid, 1)
                dve.wait_ge(s_used, t * NDVE + NDVE)
                for h in range(2):
                    add_sum(t, h)
                V.tensor_tensor_reduce(vacc[:, 1], vacc[:, 0], vacc[:, 0], 1.0, 0.0, ALU.mult, ALU.add,
                                       fss[:]).then_inc(s_fss, 1)
                dve.wait_ge(s_froot, t + 1)
                link(V.reciprocal(frs[:], frs[:]))
                link(V.scalar_tensor_tensor(out=vacc[:, 0], in0=vacc[:, 0], scalar=frs[:, 0:1],
                                             in1=rows[ROW_GT2], op0=ALU.mult, op1=ALU.mult))
                V.tensor_tensor(vacc[:, 0], vacc[:, 0], x1[:, bass.ds(t, 1), :].rearrange("p a d -> p (a d)"),
                                ALU.add).then_inc(s_fin, 1)

            PICKS_ALL = [n * (NE // 9) for n in range(PH)]
            PICKS = [n * (NE // 8) for n in range(PH - 2)]
            PER_TILE = 5 * (NQ + PH) + 9 * PH + 8
            first_dots()
            weighted_rows(0, True, PICKS_ALL)
            start = count[0]
            count[0] = 0
            with dve.Fori(1, LT - 1) as t:
                base[0] = t * PER_TILE + (start - PER_TILE)
                later_dots(t, True)
                weighted_rows(t, True, PICKS)
                assert count[0] == PER_TILE, count[0]
            base[0] = (LT - 2) * PER_TILE + start
            count[0] = 0
            later_dots(LT - 1, False)
            weighted_rows(LT - 1, False, [])


_INS = ["x", "c", "ctx", "c_ctx", "w_ada", "b_ada", "g_pre_mix", "g_post_mix", "g_pre_ffn", "g_post_ffn",
        "w_in", "ssd_conv_w", "ssd_conv_b", "ssd_dt_bias", "ssd_a_log", "ssd_d", "ssd_norm_g",
        "sc_conv_w", "sc_norm_g", "w_out", "peer_w_q", "peer_keys", "peer_u", "peer_v"]


def kernel(**inputs):
    import numpy as np
    import concourse.bacc as bacc
    from concourse.bass_utils import run_bass_kernel_spmd

    nc = bacc.Bacc("TRN2", target_bir_lowering=False, num_devices=1)
    arrays, args = {}, []
    for name in _INS:
        a = np.ascontiguousarray(inputs[name])
        arrays[f"in_{name}"] = a
        args.append(nc.dram_tensor(f"in_{name}", a.shape, mybir.dt.from_np(a.dtype), kind="ExternalInput").ap())
    out = nc.dram_tensor("out", inputs["x"].shape, F32, kind="ExternalOutput").ap()
    build(nc, *args, out)
    r = run_bass_kernel_spmd(nc, [arrays], core_ids=[0])
    return r.results[0]["out"]
```
